# Optimizing a Trainium2 kernel written in Bass

```python
import math
import jax
import jax.numpy as jnp
from jax import lax
import numpy as np

D_MODEL = 1024
BATCH = 1
SEQ = 512
DEPTH = 1
DEC_BATCH = 8
DEC_SEQ = 8
PAST_LEN = 2048
PAGE_SIZE = 128

A_GROUPS = ((128, 1), (512, 4), (2048, 16))
A_HEADS = 4
A_HEAD_DIM = 128
A_QKV = len(A_GROUPS) * A_HEADS * A_HEAD_DIM
A_OUT = A_HEADS * A_HEAD_DIM
Q_BLOCK = 128
R_HEADS = 4
R_KEY_DIM = 128
R_VAL_DIM = 256
R_QK = R_HEADS * R_KEY_DIM
R_V = R_HEADS * R_VAL_DIM
R_CHUNK = 128
ROPE_BASE = 10000.0
EPS = 1e-5
NEG_INF = -1e30
DEEPNORM_ALPHA = (2 * DEPTH) ** 0.25
DEEPNORM_BETA = (8 * DEPTH) ** -0.25
SPLIT_SIZES = (A_QKV, A_QKV, A_QKV, A_OUT, R_QK, R_QK, R_V, R_V, D_MODEL, D_MODEL)
D_IN = sum(SPLIT_SIZES)
SPLIT_POINTS = tuple(int(s) for s in np.cumsum(SPLIT_SIZES)[:-1])

kernel_name = 'dilated_retention_hybrid_step'

def alibi_slopes(n):
    return jnp.exp2(-8.0 * jnp.arange(1, n + 1, dtype=jnp.float32) / n)

def rotary(x, pos):
    half = x.shape[-1] // 2
    inv = 1.0 / (ROPE_BASE ** jnp.linspace(0.0, 1.0, half, dtype=jnp.float32))
    ang = pos.astype(jnp.float32)[:, None] * inv[None, :]
    cos = jnp.cos(ang)[None, :, None, :]
    sin = jnp.sin(ang)[None, :, None, :]
    x1, x2 = x[..., :half], x[..., half:]
    return jnp.concatenate([x1 * cos - x2 * sin, x1 * sin + x2 * cos], axis=-1)

def dilated_mixture_attention(q, ext_k, ext_v, buf_lens):
    B, T, G, H, dh = q.shape
    qb = Q_BLOCK if T % Q_BLOCK == 0 else T
    n_blk = T // qb
    slopes = alibi_slopes(G * H).reshape(G, H)
    scale = dh ** -0.5

    def block(bi):
        t0 = bi * qb
        qblk = lax.dynamic_slice_in_dim(q, t0, qb, axis=1).astype(jnp.float32)
        lses, outs = [], []
        for g, (w, d) in enumerate(A_GROUPS):
            nk = w // d + 1
            dist = jnp.arange(nk, dtype=jnp.int32) * d
            idx = buf_lens[g] + t0 + jnp.arange(qb, dtype=jnp.int32)[:, None] - dist[None, :]
            valid = idx >= 0
            idx = jnp.maximum(idx, 0)
            kg = jnp.take(ext_k[g], idx, axis=1).astype(jnp.float32)
            vg = jnp.take(ext_v[g], idx, axis=1).astype(jnp.float32)
            s = (jnp.einsum('bqhd,bqkhd->bhqk', qblk[:, :, g], kg) * scale
                 - slopes[g][None, :, None, None] * dist.astype(jnp.float32)[None, None, None, :])
            s = jnp.where(valid[None, None], s, NEG_INF)
            lse = jax.nn.logsumexp(s, axis=-1)
            p = jnp.exp(s - lse[..., None])
            outs.append(jnp.einsum('bhqk,bqkhd->bqhd', p, vg))
            lses.append(lse)
        wts = jax.nn.softmax(jnp.stack(lses, axis=0), axis=0)
        return jnp.einsum('gbhq,gbqhd->bqhd', wts, jnp.stack(outs, axis=0))

    o = lax.map(block, jnp.arange(n_blk, dtype=jnp.int32))
    return o.transpose(1, 0, 2, 3, 4).reshape(B, T, H, dh)

def retention_chunkwise(q, k, v, s0):
    B, T, H, dk = q.shape
    dv = v.shape[-1]
    c = R_CHUNK if T % R_CHUNK == 0 else T
    n = T // c
    lg = jnp.log1p(-jnp.exp2(-5.0 - jnp.arange(H, dtype=jnp.float32)))
    i = jnp.arange(c, dtype=jnp.float32)
    diff = i[:, None] - i[None, :]
    causal = diff >= 0
    dmat = jnp.where(causal[None], jnp.exp(jnp.where(causal, diff, 0.0)[None] * lg[:, None, None]), 0.0)
    q_decay = jnp.exp((i[:, None] + 1.0) * lg[None, :])
    k_decay = jnp.exp((c - 1.0 - i)[:, None] * lg[None, :])
    chunk_decay = jnp.exp(c * lg)

    def to_chunks(a):
        return a.reshape(B, n, c, H, a.shape[-1]).transpose(1, 0, 2, 3, 4)

    def step(S, qkv):
        qc, kc, vc = qkv
        att = jnp.einsum('bihd,bjhd->bhij', qc, kc) * dmat[None]
        o = (jnp.einsum('bhij,bjhe->bihe', att, vc)
             + jnp.einsum('bihd,bhde->bihe', qc, S) * q_decay[None, :, :, None])
        S = (chunk_decay[None, :, None, None] * S
             + jnp.einsum('bjhd,bjhe->bhde', kc * k_decay[None, :, :, None], vc))
        return S, o

    S, o = lax.scan(step, s0, (to_chunks(q), to_chunks(k), to_chunks(v)))
    return o.transpose(1, 0, 2, 3, 4).reshape(B, T, H, dv), S

def hybrid_layer(x, pos0, bufs, s0, w_in, w_pa, w_pb, w_o, gn_g, ln_g, ln_b):
    B, T, _ = x.shape
    G = len(A_GROUPS)
    h = x @ w_in
    qa, ka, va, za, qr, kr, vr, zr, ga, gb = jnp.split(h, SPLIT_POINTS, axis=-1)
    qa = qa.reshape(B, T, G, A_HEADS, A_HEAD_DIM)
    ka = ka.reshape(B, T, G, A_HEADS, A_HEAD_DIM)
    va = va.reshape(B, T, G, A_HEADS, A_HEAD_DIM)
    ext_k, ext_v, lens, new_bufs = [], [], [], []
    for g, (w, d) in enumerate(A_GROUPS):
        kv_new = jnp.stack([ka[:, :, g], va[:, :, g]], axis=2)
        if bufs is None:
            kv_all = kv_new
            lens.append(0)
        else:
            kv_all = jnp.concatenate([bufs[g].astype(kv_new.dtype), kv_new], axis=1)
            lens.append(bufs[g].shape[1])
        ext_k.append(kv_all[:, :, 0])
        ext_v.append(kv_all[:, :, 1])
        keep = min(w, kv_all.shape[1])
        new_bufs.append(kv_all[:, kv_all.shape[1] - keep:])
    o_a = dilated_mixture_attention(qa, ext_k, ext_v, lens)
    pos = pos0 + jnp.arange(T, dtype=jnp.int32)
    qr = rotary(qr.reshape(B, T, R_HEADS, R_KEY_DIM).astype(jnp.float32), pos)
    kr = rotary(kr.reshape(B, T, R_HEADS, R_KEY_DIM).astype(jnp.float32), pos) * (R_KEY_DIM ** -0.5)
    vr = vr.reshape(B, T, R_HEADS, R_VAL_DIM).astype(jnp.float32)
    o_r, s_new = retention_chunkwise(qr, kr, vr, s0.astype(jnp.float32))
    mu = jnp.mean(o_r, axis=-1, keepdims=True)
    var = jnp.mean(jnp.square(o_r - mu), axis=-1, keepdims=True)
    o_r = ((o_r - mu) * lax.rsqrt(var + EPS)).reshape(B, T, R_V) * gn_g.astype(jnp.float32)
    y_a = (jax.nn.silu(za) * o_a.reshape(B, T, A_OUT).astype(x.dtype)) @ w_pa
    y_b = (jax.nn.silu(zr) * o_r.astype(x.dtype)) @ w_pb
    out = (jax.nn.sigmoid(ga) * y_a + jax.nn.sigmoid(gb) * y_b) @ w_o
    z = (DEEPNORM_ALPHA * x + out).astype(jnp.float32)
    zm = jnp.mean(z, axis=-1, keepdims=True)
    zv = jnp.mean(jnp.square(z - zm), axis=-1, keepdims=True)
    y = ((z - zm) * lax.rsqrt(zv + EPS) * ln_g.astype(jnp.float32) + ln_b.astype(jnp.float32)).astype(x.dtype)
    return y, new_bufs[0], new_bufs[1], new_bufs[2], s_new.astype(x.dtype)

def setup_inputs(seed: int = 0) -> dict:
    key = jax.random.key(seed)
    ks = jax.random.split(key, 16)
    f32 = jnp.float32
    x_prompt = jax.random.normal(ks[0], (BATCH, SEQ, D_MODEL), f32)
    x_sample = jax.random.normal(ks[1], (DEC_BATCH, DEC_SEQ, D_MODEL), f32)
    caches = [jax.random.normal(ks[2 + g], (DEC_BATCH, min(w, PAST_LEN), 2, A_HEADS, A_HEAD_DIM), f32)
              for g, (w, _) in enumerate(A_GROUPS)]
    state_ret = 0.5 * jax.random.normal(ks[5], (DEC_BATCH, R_HEADS, R_KEY_DIM, R_VAL_DIM), f32)
    offs = np.concatenate([[0], np.cumsum(SPLIT_SIZES)])
    col_scale = np.ones((D_IN,), np.float32)
    col_scale[offs[2]:offs[3]] = DEEPNORM_BETA
    col_scale[offs[6]:offs[7]] = DEEPNORM_BETA
    w_in = jax.random.normal(ks[6], (D_MODEL, D_IN), f32) * (D_MODEL ** -0.5) * jnp.asarray(col_scale)
    w_pa = jax.random.normal(ks[7], (A_OUT, D_MODEL), f32) * (A_OUT ** -0.5) * DEEPNORM_BETA
    w_pb = jax.random.normal(ks[8], (R_V, D_MODEL), f32) * (R_V ** -0.5) * DEEPNORM_BETA
    w_o = jax.random.normal(ks[9], (D_MODEL, D_MODEL), f32) * (D_MODEL ** -0.5) * DEEPNORM_BETA
    gn_g = 1.0 + 0.02 * jax.random.normal(ks[10], (R_V,), f32)
    ln_g = 1.0 + 0.02 * jax.random.normal(ks[11], (D_MODEL,), f32)
    ln_b = 0.02 * jax.random.normal(ks[12], (D_MODEL,), f32)
    return {'x_prompt': x_prompt, 'x_sample': x_sample,
            'cache_kv_w128': caches[0], 'cache_kv_w512': caches[1], 'cache_kv_w2048': caches[2],
            'state_ret': state_ret,
            'w_in': w_in, 'w_pa': w_pa, 'w_pb': w_pb, 'w_o': w_o,
            'gn_g': gn_g, 'ln_g': ln_g, 'ln_b': ln_b}

def reference(x_prompt, x_sample, cache_kv_w128, cache_kv_w512, cache_kv_w2048, state_ret,
              w_in, w_pa, w_pb, w_o, gn_g, ln_g, ln_b):
    y_p, x_p = x_prompt, x_prompt
    y_s, x_s = x_sample, x_sample
    for layer in range(DEPTH):
        s0_p = jnp.zeros((x_p.shape[0], R_HEADS, R_KEY_DIM, R_VAL_DIM), jnp.float32)
        y_p, kv128_p, kv512_p, kv2048_p, ret_p = hybrid_layer(
            x_p, 0, None, s0_p, w_in, w_pa, w_pb, w_o, gn_g, ln_g, ln_b)
        y_s, kv128_s, kv512_s, kv2048_s, ret_s = hybrid_layer(
            x_s, PAST_LEN, (cache_kv_w128, cache_kv_w512, cache_kv_w2048), state_ret,
            w_in, w_pa, w_pb, w_o, gn_g, ln_g, ln_b)
        x_p, x_s = y_p, y_s
    return (y_p, y_s, kv128_p, kv512_p, kv2048_p, ret_p, kv128_s, kv512_s, kv2048_s, ret_s)


_drawn_inputs = setup_inputs


def setup_inputs(seed=0):
    import zlib

    import numpy as np

    out = dict(_drawn_inputs(seed))
    spreads = {}
    factors = {}
    for name, (base, spread) in spreads.items():
        noise = np.random.default_rng([zlib.crc32(name.encode()), seed]).standard_normal(out[name].shape)
        drawn = base * np.exp(spread * noise) if base else spread * noise
        out[name] = jnp.asarray(drawn.astype(out[name].dtype))
    for name, factor in factors.items():
        out[name] = (out[name] * factor).astype(out[name].dtype)
    return out
```

```python
import math
from contextlib import ExitStack

import numpy as np

import concourse.bass as bass
from concourse import mybir

F32 = mybir.dt.float32
F32R = mybir.dt.float32r
ALU = mybir.AluOpType
ACT = mybir.ActivationFunctionType
AX = mybir.AxisListType

P = 128
D_MODEL, D_IN = 1024, 10240
KT_N = D_MODEL // P
SEQ, DEC_B, DEC_T = 512, 8, 8
NS = DEC_B * DEC_T
NTOK = NS + SEQ
QBLK = SEQ // P
TT = QBLK + 1
HALF = NTOK // 2
GROUPS = ((128, 1), (512, 4), (2048, 16))
G, H, DH = 3, 4, 128
RH, RK, RV = 4, 128, 256
A_QKV, A_OUT = G * H * DH, H * DH
OFF_Q, OFF_K, OFF_V = 0, A_QKV, 2 * A_QKV
OFF_ZA = 3 * A_QKV
OFF_QR = OFF_ZA + A_OUT
OFF_KR = OFF_QR + RH * RK
OFF_VR = OFF_KR + RH * RK
OFF_ZR = OFF_VR + RH * RV
OFF_GA = OFF_ZR + RH * RV
OFF_GB = OFF_GA + D_MODEL
SCALE = DH ** -0.5
EPS = 1e-5
ALPHA = 2 ** 0.25
PAST = 2048
MASKED = -1e32
CW = 256
HW = KT_N * CW // 2
A_CH, B_CH, C_CH = 6, 2, 2
UD, TD = 5, 6
C0_B = H * A_CH
C0_C = C0_B + RH * B_CH
C0_O = C0_C + KT_N * C_CH
ZR_UNIT = 23
A_UNITS = 27
B_UNITS = 10
A_TG, B_TG = 14, 26
U_B = H * A_UNITS
TG_B = TD + H * A_TG
TB_B = H * A_TG // 2
A_COPY_B = 5
ROWS = H * DEC_T
ND_W = (256, 512, 512)
ND_O = (0, 256, 768)

_W = [("ident", P), ("slopes", 12), ("biasc", 384), ("biasn", 360), ("cos", TT * 64), ("sin", TT * 64),
      ("dmat", RH * P), ("dmats", RH * NS), ("qdec", RH * P), ("qdecs", RH * NS), ("kdec", RH * TT),
      ("cdec", RH * 2), ("bmask", DEC_B)]
COL, _o = {}, 0
for _n, _w in _W:
    COL[_n] = (_o, _w)
    _o += _w
NCONST = _o


def shape_constants():
    c = np.zeros((P, NCONST), np.float32)

    def put(name, a):
        o, w = COL[name]
        a = np.asarray(a, np.float32).reshape(a.shape[0], w)
        c[:a.shape[0], o:o + w] = a

    put("ident", np.eye(P))
    slope = 2.0 ** (-8.0 * np.arange(1, G * H + 1) / (G * H)).reshape(G, H)
    put("slopes", np.broadcast_to(slope.T.reshape(1, G * H), (P, G * H)))
    bc = np.zeros((H, DEC_T, G, P))
    bn = np.zeros((H, DEC_T, G, 120))
    m = np.arange(P)
    t = np.arange(120) - 56
    for q in range(DEC_T):
        idx = (m, 4 * m + q % 4, 16 * m + q)
        for g, (w, d) in enumerate(GROUPS):
            dist = w + q - idx[g]
            new = q - t
            ok = (t >= 0) & (new >= 0) & (new % d == 0)
            for h in range(H):
                bc[h, q, g] = np.where(dist <= w, -slope[g, h] * dist, MASKED)
                bn[h, q, g] = np.where(ok, -slope[g, h] * new, MASKED)
    put("biasc", bc.reshape(H * DEC_T, -1))
    put("biasn", bn.reshape(H * DEC_T, -1))
    f32 = np.float32
    frac = np.arange(64, dtype=f32) * (f32(1) / f32(63))
    inv = (f32(1) / (10000.0 ** frac.astype(np.float64)).astype(f32)).astype(f32)
    pos = np.zeros((P, TT), np.float32)
    for k in range(QBLK):
        pos[:, k] = k * P + np.arange(P)
    pos[:, QBLK] = PAST + np.arange(P) % DEC_T
    ang = (pos[:, :, None] * inv).astype(np.float32).astype(np.float64)
    put("cos", np.cos(ang))
    put("sin", np.sin(ang))
    lg = np.log1p(-np.exp2(-5.0 - np.arange(RH)))
    i = np.arange(P)
    diff = i[None, :] - i[:, None]
    ks = RK ** -0.5
    put("dmat", (np.where(diff >= 0, np.exp(np.maximum(diff, 0) * lg[:, None, None]), 0) * ks).transpose(1, 0, 2))
    j = np.arange(NS)
    ds = j[None, :] - j[:, None]
    same = (j[None, :] // DEC_T == j[:, None] // DEC_T) & (ds >= 0)
    put("dmats", (np.where(same, np.exp(np.maximum(ds, 0) * lg[:, None, None]), 0) * ks).transpose(1, 0, 2))
    put("qdec", np.broadcast_to(np.exp((i + 1) * lg[:, None]), (P, RH, P)))
    put("qdecs", np.broadcast_to(np.exp((j % DEC_T + 1) * lg[:, None]), (P, RH, NS)))
    kd = np.zeros((P, RH, TT))
    for r in range(RH):
        kd[:, r, :QBLK] = (np.exp((P - 1.0 - i) * lg[r]) * ks)[:, None]
        kd[:, r, QBLK] = np.exp((DEC_T - 1.0 - i % DEC_T) * lg[r]) * ks
    put("kdec", kd)
    put("cdec", np.broadcast_to(np.stack([np.exp(P * lg), np.exp(DEC_T * lg)], 1), (P, RH, 2)))
    put("bmask", (i[:NS, None] // DEC_T == np.arange(DEC_B)[None]).astype(np.float32))
    nd = np.zeros((P, sum(ND_W)), np.float32)
    for g, (w, d) in enumerate(GROUPS):
        x = np.arange(ND_W[g]) - (ND_W[g] - P)
        dist = i[:, None] - x[None, :]
        ok = (dist >= 0) & (dist <= w) & (dist % d == 0)
        nd[:, ND_O[g]:ND_O[g] + ND_W[g]] = np.where(ok, -dist, MASKED)
    return c, nd


def unit_bank(u):
    return (u + (u >= ZR_UNIT)) % 2


class Links:

    def __init__(self, eng, sem):
        self.eng, self.sem, self.base, self.n, self.turn, self.per = eng, sem, 0, 0, None, 0

    def enter(self, turn, per):
        self.base, self.turn, self.per, self.n = self.base + self.n, turn, per, 0

    def leave(self, turns):
        assert self.n == self.per, f"links per turn: {self.n}, not {self.per}"
        self.base, self.turn, self.n = self.base + turns * self.per, None, 0

    def after(self, ins):
        ins.then_inc(self.sem, 1)
        self.n += 1
        v = self.base + self.n
        self.eng.wait_ge(self.sem, v if self.turn is None else self.turn * self.per + v)


def bass_hybrid_step(nc, x_prompt, x_sample, cache128, cache512, cache2048, state_ret, w_in, w_pa, w_pb, w_o,
                     gn_t, ln_g, ln_b, consts, dist_tab,
                     y_prompt, y_sample, kv128_p, kv512_p, kv2048_p, ret_p, kv128_s, kv512_s, kv2048_s, ret_s):
    caches = (cache128, cache512, cache2048)
    kv_p = (kv128_p, kv512_p, kv2048_p)
    kv_s = (kv128_s, kv512_s, kv2048_s)

    with ExitStack() as ctx:
        def sb(name, shape, dt=F32, scope=ctx):
            return scope.enter_context(nc.sbuf_tensor(name, shape, dt))

        def sem(name):
            return ctx.enter_context(nc.semaphore(name))

        bank = [ctx.enter_context(nc.psum_tensor(f"bank{b}", [P, 512], F32)) for b in range(8)]

        xh = sb("xh", [P, KT_N, NTOK], F32R)
        xl = sb("xl", [P, KT_N, NTOK], F32R)
        wraw = [sb(f"wraw{s}", [P, HW]) for s in range(2)]
        wh = [sb(f"wh{b}", [P, 2 * HW], F32R) for b in range(2)]
        wl = [sb(f"wl{b}", [P, 2 * HW], F32R) for b in range(2)]
        con = sb("con", [P, NCONST])
        gn = sb("gn", [P, RH * RV // P])

        def const(name, parts=P):
            o, w = COL[name]
            return con[0:parts, o:o + w]

        ident = const("ident")
        scope_c = ExitStack()
        scope_ab = ExitStack()
        oa = sb("oa", [P, H * NTOK], F32, scope_ab)
        yb = sb("yb", [P, 2 * RH * NTOK], F32, scope_ab)
        qts = sb("qts", [P, H * G * NS], F32, scope_ab)
        ktn = sb("ktn", [P, H * G * NS], F32, scope_ab)
        vn = sb("vn", [NS, H * G * DH], F32, scope_ab)
        scope_x = ExitStack()
        xn = sb("xn", [P, TT, D_MODEL], F32, scope_x)
        scope_x.close()
        scope_a = ExitStack()
        kv = sb("kv", [P, QBLK, 2 * G * DH], F32, scope_a)
        ks = sb("ks", [NS, G * DH], F32, scope_a)
        kt = sb("kt", [P, G, SEQ], F32, scope_a)
        qt = sb("qt", [P, G, SEQ], F32, scope_a)
        sp_ = sb("scoresp", [P, 2, 1280], F32, scope_a)
        pt = sb("pt", [P, 2, 1280], F32, scope_a)
        on = sb("on", [P, QBLK, DH], F32, scope_a)
        sg = sb("sg", [P, 2, HALF], F32, scope_a)
        nd = sb("nd", [P, sum(ND_W)], F32, scope_a)
        nmax = sb("nmax", [P, QBLK], F32, scope_a)
        rsum = sb("rsum", [P, QBLK], F32, scope_a)
        rinv = sb("rinv", [P, QBLK], F32, scope_a)
        scope_a.close()
        scope_b = ExitStack()
        cslot = [sb(f"cslot{s}", [P, n, H * DH], F32, scope_b) for s, n in enumerate((5, 4, 4))]
        ckt = sb("ckt", [P, 2, H * P], F32, scope_b)
        qk = sb("qk", [P, TT, 2 * RK], F32, scope_b)
        rot = sb("rot", [P, TT, 2 * RK], F32, scope_b)
        kd = sb("kd", [P, TT, RK], F32, scope_b)
        vr = sb("vr", [P, TT, RV], F32, scope_b)
        qrt = sb("qrt", [P, SEQ], F32, scope_b)
        qdt = sb("qdt", [P, SEQ], F32, scope_b)
        krt = sb("krt", [P, SEQ], F32, scope_b)
        qkts = sb("qkts", [P, 2 * NS], F32, scope_b)
        qdm = sb("qdm", [P, DEC_B * NS], F32, scope_b)
        atts = sb("atts", [NS, NS], F32, scope_b)
        st = sb("st", [P, DEC_B, RV], F32, scope_b)
        schain = sb("schain", [P, QBLK, RV], F32, scope_b)
        qm = sb("qm", [P, 60 * ROWS], F32, scope_b)
        srow = sb("srow", [ROWS, 576], F32, scope_b)
        smx = sb("smx", [ROWS, 4], F32, scope_b)
        pm = sb("pm", [P, 13 * ROWS], F32, scope_b)
        pn = sb("pn", [NS, G * ROWS], F32, scope_b)
        bst = sb("bst", [P, TT, 6], F32, scope_b)
        bmv = sb("bmv", [P, TT, 2], F32, scope_b)
        rstd = sb("rstd", [P, TT], F32, scope_b)
        half = sb("half", [P, TT], F32, scope_b)
        scope_b.close()
        scope_ab.close()
        km = rot[0:NS].rearrange("p a b -> p (a b)")[:, 0:DEC_B * RK]
        uh = sb("uh", [P, KT_N, NTOK], F32R, scope_c)
        ul = sb("ul", [P, KT_N, NTOK], F32R, scope_c)
        ybh = sb("ybh", [P, 2 * RH, NTOK], F32R, scope_c)
        ybl = sb("ybl", [P, 2 * RH, NTOK], F32R, scope_c)
        oah = sb("oah", [P, H, NTOK], F32R, scope_c)
        oal = sb("oal", [P, H, NTOK], F32R, scope_c)
        sgc = sb("sgc", [P, 2, NTOK], F32, scope_c)
        uc = sb("uc", [P, 2, NTOK], F32, scope_c)
        scope_c.close()
        scope_d = ExitStack()
        sb("uh_", [P, KT_N, NTOK], F32, scope_d)
        sb("ul_", [P, KT_N, NTOK], F32, scope_d)
        z = sb("z", [P, TT, D_MODEL], F32, scope_d)
        lng = sb("lng", [P, D_MODEL], F32, scope_d)
        lnb = sb("lnb", [P, D_MODEL], F32, scope_d)
        zst = sb("zst", [P, TT, 12], F32, scope_d)
        zmv = sb("zmv", [P, TT, 2], F32, scope_d)
        zrs = sb("zrs", [P, TT], F32, scope_d)
        zhf = sb("zhf", [P, TT], F32, scope_d)
        scope_d.close()

        con_in, nd_in, gn_in, x_in = sem("con_in"), sem("nd_in"), sem("gn_in"), sem("x_in")
        passed = sem("passed")
        credits = sem("credits")
        xt_done = sem("xt_done")
        xh_done = sem("xh_done")
        xl_done = sem("xl_done")
        w_in_s = [sem(f"w_in{s}") for s in range(2)]
        w_high = sem("w_high")
        w_low = sem("w_low")
        unit_done = sem("unit_done")
        unit_free = sem("unit_free")
        gate_sig = sem("gate_sig")
        gate_free = sem("gate_free")
        tg_done = sem("tg_done")
        tg_free = [sem(f"tg_free{b}") for b in range(2)]
        score_done = sem("score_done")
        score_free = sem("score_free")
        max_done = sem("max_done")
        exp_done = sem("exp_done")
        o_done = sem("o_done")
        o_read = sem("o_read")
        k_stored, v_stored = sem("k_stored"), sem("v_stored")
        kv_out = sem("kv_out")
        states_out = sem("states_out")
        a_end, b_end = sem("a_end"), sem("b_end")
        slot_in = [sem(f"slot_in{s}") for s in range(3)]
        slot_free = [sem(f"slot_free{s}") for s in range(3)]
        qm_done = sem("qm_done")
        cs_done, rows_max, rows_exp = sem("cs_done"), sem("rows_max"), sem("rows_exp")
        cp_done, cp_read = sem("cp_done"), sem("cp_read")
        co_done, co_scaled = sem("co_done"), sem("co_scaled")
        ct_done, co_read = sem("ct_done"), sem("co_read")
        rot_done, kd_done, km_done = sem("rot_done"), sem("kd_done"), sem("km_done")
        rt_done = sem("rt_done")
        rt_free = [sem(f"rt_free{b}") for b in range(2)]
        st_in, st_stored, sc_stored = sem("st_in"), sem("st_stored"), sem("sc_stored")
        var_done, rstd_done, normed = sem("var_done"), sem("rstd_done"), sem("normed")
        split_h, split_l = sem("split_h"), sem("split_l")
        gt_done, gt_free = sem("gt_done"), sem("gt_free")
        br_done, br_free = sem("br_done"), sem("br_free")
        u_done, uh_done, ul_done = sem("u_done"), sem("uh_done"), sem("ul_done")
        z_in, ln_in = sem("z_in"), sem("ln_in")
        ou_done, ou_free = sem("ou_done"), sem("ou_free")
        zvar_done, zrstd_done, y_done = sem("zvar_done"), sem("zrstd_done"), sem("y_done")
        y_stored, s_stored, copied = sem("y_stored"), sem("s_stored"), sem("copied")
        dve_l, pool_l = sem("dve_l"), sem("pool_l")
        CREDIT = [(w_low, 2), (unit_done, 5), (unit_free, 3), (gate_free, 2), (tg_done, 6), (score_free, 1),
                  (o_read, 1), (cs_done, 1), (co_read, 1), (kv_out, 1), (states_out, 1),
                  (gt_free, 4), (br_free, 4), (br_done, 1), (u_done, 1),
                  *((x, 1) for x in (*tg_free, *rt_free, *slot_free))]

        block = ctx.enter_context(nc.Block())

        def settle(eng):
            eng.sem_inc(passed, 1)

        @block.sync
        def _(sp):
            def load_half(c, s, pieces):
                sp.wait_ge(w_low, c * 2 + s + 1)
                settle(sp)
                for dst, src in pieces:
                    sp.dma_start(dst, src).then_inc(w_in_s[s], 16 * (2 // len(pieces)))

            def columns(c, offs, width):
                for s in range(2):
                    dst = wraw[s][:, :].rearrange("p (k n) -> p k n", n=CW)
                    src = w_in.rearrange("(k p) n -> p k n", p=P)[:, 4 * s:4 * s + 4, :]
                    if width == CW:
                        pieces = [(dst, src[:, :, bass.ds(offs[0], CW)])]
                    else:
                        pieces = [(dst[:, :, n * width:(n + 1) * width], src[:, :, bass.ds(offs[n], width)])
                                  for n in range(2)]
                    load_half(c, s, pieces)

            sp.dma_start(xn[:, 0:QBLK, :], x_prompt[0].rearrange("(t p) d -> p t d", p=P)).then_inc(x_in, 16)
            sp.dma_start(xn[0:NS, QBLK, :], x_sample.rearrange("b t d -> (b t) d")).then_inc(x_in, 16)
            sp.dma_start(con[:, :], consts).then_inc(con_in, 16)
            sp.wait_ge(credits, 1)

            def rows(g, b, lo, n):
                w = GROUPS[g][0]
                src = caches[g][b].rearrange("s c h d -> s (c h d)")[DEC_T:w]
                dst = kv_s[g][b].rearrange("s c h d -> s (c h d)")[0:w - DEC_T]
                sp.dma_start(dst[bass.ds(lo, n), :], src[bass.ds(lo, n), :]).then_inc(copied, 16)

            def stage_a(h):
                cols = [(OFF_K, OFF_K + 512), (OFF_K + 1024, OFF_V), (OFF_Q, OFF_Q + 512), (OFF_Q + 1024, OFF_ZA),
                        (OFF_V + 512, OFF_V + 1024)]
                for j, (a, b) in enumerate(cols):
                    columns(h * A_CH + j, (h * DH + a, h * DH + b), DH)
                    rows(2, j, h * 510, 510)
                columns(h * A_CH + 5, (h * RV + OFF_ZR,), CW)
                for b in range(A_COPY_B):
                    rows(1, b, h * 126, 126)
                    rows(0, b, h * 30, 30)

            with sp.Fori(0, H) as h:
                stage_a(h)

            sp.dma_start(gn[:, :], gn_t).then_inc(gn_in, 16)

            def retention_chunk(c, r, which):
                if which == 0:
                    columns(c, (r * RK + OFF_QR, r * RK + OFF_KR), RK)
                else:
                    columns(c, (r * RV + OFF_VR,), CW)

            def load_cache(b, which, tiles):
                views = [caches[g].rearrange("b (m d) c h e -> b m d c (h e)", d=GROUPS[g][1]) for g in range(G)]

                def pick(g, lo, k):
                    return views[g][bass.ds(b, 1), :, lo:lo + k, which, :].rearrange("b m d e -> m (b d) e")

                def free(s):
                    if which:
                        sp.wait_ge(tg_done, tiles + (TG_B + (5, 9, 13)[s]))
                    else:
                        sp.wait_ge(slot_free[s], b + 1)

                free(0)
                sp.dma_start(cslot[0][:, 0:1, :], pick(0, 0, 1)).then_inc(slot_in[0], 16)
                sp.dma_start(cslot[0][:, 1:5, :], pick(1, 0, 4)).then_inc(slot_in[0], 16)
                for s in (1, 2):
                    free(s)
                    sp.dma_start(cslot[s][:, :, :], pick(2, 4 * s - 4, 4)).then_inc(slot_in[s], 32)

            retention_chunk(C0_B, 0, 0)
            sp.wait_ge(a_end, 4)

            def gate_chunk(c, f):
                columns(c, (f * P + OFF_GA, f * P + OFF_GB), P)

            def stage_b(r, last):
                retention_chunk(r * B_CH + (C0_B + 1), r, 1)
                load_cache(r * 2, 0, 0)
                sp.wait_ge(states_out, r + 1)
                sp.dma_start(st[:, :, :], state_ret[:, bass.ds(r, 1), :, :].rearrange("b r d e -> d (b r) e"))\
                    .then_inc(st_in, 16)
                load_cache(r * 2, 1, r * B_TG)
                if last:
                    gate_chunk(C0_C, 0)
                else:
                    retention_chunk(r * B_CH + (C0_B + 2), r + 1, 0)
                load_cache(r * 2 + 1, 0, 0)
                load_cache(r * 2 + 1, 1, r * B_TG + 13)

            with sp.Fori(0, RH - 1) as r:
                stage_b(r, False)
            stage_b(RH - 1, True)

            def branch_chunk(c, f):
                pa = w_pa.rearrange("(k p) n -> p k n", p=P)[:, :, bass.ds(f * P, P)]
                pb = w_pb.rearrange("(k p) n -> p k n", p=P)[:, :, bass.ds(f * P, P)]
                d = [wraw[s][:, 0:6 * P].rearrange("p (k n) -> p k n", n=P) for s in range(2)]
                load_half(c, 0, [(d[0][:, 0:4, :], pa), (d[0][:, 4:6, :], pb[:, 0:2, :])])
                load_half(c, 1, [(d[1], pb[:, 2:8, :])])

            def out_chunk(c, n):
                src = w_o.rearrange("(k p) n -> p k n", p=P)
                for s in range(2):
                    dst = wraw[s][:, :].rearrange("p (k n) -> p k n", n=CW)
                    load_half(c, s, [(dst, src[:, 4 * s:4 * s + 4, n * CW:(n + 1) * CW])])

            def stage_c(f, last):
                branch_chunk(f * C_CH + (C0_C + 1), f)
                for b in range(A_COPY_B, DEC_B):
                    rows(2, b, f * 255, 255)
                if last:
                    out_chunk(C0_O, 0)
                else:
                    gate_chunk(f * C_CH + (C0_C + 2), f + 1)
                for b in range(A_COPY_B, DEC_B):
                    rows(1, b, f * 63, 63)
                    rows(0, b, f * 15, 15)

            with sp.Fori(0, KT_N - 1) as f:
                stage_c(f, False)
            stage_c(KT_N - 1, True)
            for n in range(1, 4):
                out_chunk(C0_O + n, n)
                if n == 1:
                    sp.wait_ge(br_free, 4 + 4 * KT_N)
                    sp.dma_start(z[:, 0:QBLK, :], x_prompt[0].rearrange("(t p) d -> p t d", p=P)).then_inc(z_in, 16)
                    sp.dma_start(z[0:NS, QBLK, :], x_sample.rearrange("b t d -> (b t) d")).then_inc(z_in, 16)
                    for dst, src in ((lng, ln_g), (lnb, ln_b)):
                        sp.dma_start(dst[:, :], src.rearrange("(a d) -> a d", a=1).to_broadcast([P, D_MODEL]))\
                            .then_inc(ln_in, 16)
            sp.wait_ge(copied, 16 * (H * (5 + 2 * A_COPY_B) + KT_N * 3 * (DEC_B - A_COPY_B)))

        @block.gpsimd
        def _(pool):
            own = Links(pool, pool_l)
            tt = pool.tensor_tensor
            for s, n in CREDIT:
                pool.sem_inc(s, n)
            pool.sem_inc(credits, 1)
            pool.dma_start(nd[:, :], dist_tab).then_inc(nd_in, 16)

            def store_kv(h, which):
                done = k_stored if which == 0 else v_stored
                for g in range(G):
                    w = GROUPS[g][0]
                    o = (which * G + g) * DH
                    lo = QBLK - 1 if g == 0 else 0
                    dst = kv_p[g][0].rearrange("(t p) c h d -> p t c h d", p=P)[:, :, which, bass.ds(h, 1), :]
                    pool.dma_start(dst.rearrange("p t h d -> p t (h d)"), kv[:, lo:QBLK, o:o + DH]).then_inc(done, 16)
                    dst = kv_s[g][:, w - DEC_T:w, which, bass.ds(h, 1), :].rearrange("b t h d -> b t (h d)")
                    src = ks[:, g * DH:(g + 1) * DH] if which == 0 else vn[:, bass.ds(h * (G * DH) + g * DH, DH)]
                    pool.dma_start(dst, src).then_inc(done, 16)

            with pool.Fori(0, H) as h:
                pool.wait_ge(unit_free, h * A_UNITS + (3 + 10))
                store_kv(h, 0)
                pool.wait_ge(unit_free, h * A_UNITS + (3 + 23))
                store_kv(h, 1)
                pool.wait_ge(k_stored, h * 96 + 96)
                pool.wait_ge(v_stored, h * 96 + 96)
                pool.sem_inc(kv_out, 1)
            pool.sem_inc(a_end, 1)
            pool.wait_ge(a_end, 4)
            own.after(pool.memset(qk[NS:P, QBLK, :], 0.0))
            own.after(pool.memset(half[:, :], -0.5))
            own.after(pool.memset(qm[:, :], 0.0))
            own.after(pool.memset(pm[:, :], 0.0))
            pool.memset(qdm[:, :], 0.0).then_inc(kd_done, 1)
            pool.wait_ge(kd_done, 1)
            pool.wait_ge(con_in, 16)

            x1, x2 = (qk[:, :, :].rearrange("p t (c e) -> p t c e", c=2)[:, :, :, 64 * n:64 * n + 64] for n in range(2))
            y1, y2 = (rot[:, :, :].rearrange("p t (c e) -> p t c e", c=2)[:, :, :, 64 * n:64 * n + 64] for n in range(2))
            tm = kd[:, :, :].rearrange("p t (c e) -> p t c e", c=2)
            cs, sn = (const(n).rearrange("p (t a e) -> p t a e", a=1, e=64).to_broadcast([P, TT, 2, 64])
                      for n in ("cos", "sin"))
            with pool.Fori(0, RH) as r:
                own.enter(r, 7)
                pool.wait_ge(unit_free, r * B_UNITS + (3 + U_B + 5))
                pool.wait_ge(rt_free[1], r * 9 + 1)
                tt(y1, x1, cs, ALU.mult)
                own.after(tt(tm, x2, sn, ALU.mult))
                own.after(tt(y1, y1, tm, ALU.subtract))
                tt(y2, x1, sn, ALU.mult)
                own.after(tt(tm, x2, cs, ALU.mult))
                tt(y2, y2, tm, ALU.add).then_inc(rot_done, 1)
                pool.wait_ge(rot_done, r + 1)
                kdec = const("kdec")[:, bass.ds(r * TT, TT)].rearrange("p (t a) -> p t a", a=1).to_broadcast([P, TT, RK])
                tt(kd[:, :, :], rot[:, :, RK:2 * RK], kdec, ALU.mult).then_inc(kd_done, 1)
                pool.wait_ge(kd_done, r + 2)
                pool.wait_ge(rt_done, r * 18 + 3)
                tt(km.rearrange("p (b e) -> p b e", e=RK), kd[0:NS, QBLK:TT, :].to_broadcast([NS, DEC_B, RK]),
                   const("bmask", NS).rearrange("p (b a) -> p b a", a=1).to_broadcast([NS, DEC_B, RK]),
                   ALU.mult).then_inc(km_done, 1)
                pool.wait_ge(var_done, r + 1)
                settle(pool)
                own.after(pool.tensor_scalar(rstd[:, 0:QBLK], bmv[:, 0:QBLK, 1], EPS, None, ALU.add))
                own.after(tt(rstd[:, 0:QBLK], rstd[:, 0:QBLK], half[:, 0:QBLK], ALU.pow))
                settle(pool)
                own.after(pool.tensor_scalar(rstd[0:NS, QBLK:TT], bmv[0:NS, QBLK, 1:2], EPS, None, ALU.add))
                tt(rstd[0:NS, QBLK:TT], rstd[0:NS, QBLK:TT], half[0:NS, QBLK:TT], ALU.pow).then_inc(rstd_done, 1)
                own.after(pool.memset(half[:, 0:1], -0.5))
                pool.wait_ge(rt_free[1], r * 9 + 4)
                settle(pool)
                pool.dma_start(ret_p[0, bass.ds(r, 1), :, :].rearrange("r d e -> d (r e)"), schain[:, QBLK - 1, :])\
                    .then_inc(sc_stored, 16)
                for n in range(4):
                    pool.wait_ge(rt_free[n % 2], r * 9 + (7 + n // 2))
                    settle(pool)
                    dst = ret_s[2 * n:2 * n + 2, bass.ds(r, 1), :, :].rearrange("b r d e -> d (b r) e")
                    pool.dma_start(dst, st[:, 2 * n:2 * n + 2, :]).then_inc(st_stored, 16)
                pool.wait_ge(st_stored, r * 64 + 64)
                pool.wait_ge(sc_stored, r * 16 + 16)
                pool.sem_inc(states_out, 1)
            own.leave(RH)
            pool.sem_inc(b_end, 1)

            pool.wait_ge(br_free, 4 + 4 * KT_N)
            own.after(pool.memset(zhf[:, :], -0.5))
            for t in range(TT):
                m = P if t < QBLK else NS
                pool.wait_ge(zvar_done, t + 1)
                own.after(pool.tensor_scalar(zrs[0:m, t:t + 1], zmv[0:m, t, 1:2], EPS, None, ALU.add))
                tt(zrs[0:m, t:t + 1], zrs[0:m, t:t + 1], zhf[0:m, t:t + 1], ALU.pow).then_inc(zrstd_done, 1)

        @block.tensor
        def _(pe):
            def turn(out, in_):
                k = in_.shape[0]
                return pe.transpose(out, in_, ident[0:k, 0:k])

            def mm3(out, lhs, rhs, n):
                for k in range(n):
                    pe.matmul(out, lhs[0](k), rhs[0](k), start=(k == 0), stop=False)
                    pe.matmul(out, lhs[0](k), rhs[1](k), start=False, stop=False)
                    last = pe.matmul(out, lhs[1](k), rhs[0](k), start=False, stop=(k == n - 1))
                return last

            def tok(t):
                return slice(NS + t * P, NS + (t + 1) * P) if t < QBLK else slice(0, P)

            def chunk_ready(c):
                pe.wait_ge(w_low, c * 2 + 4)

            def weights(par, lo, n, width=CW):
                return [(lambda k, a=a: a[par][:, k * width + lo:k * width + lo + n]) for a in (wh, wl)]

            def halves(hi, lo, s):
                return [(lambda k, a=a: a[:, k, s * HALF:(s + 1) * HALF]) for a in (hi, lo)]

            def tiles(hi, lo, t):
                return [(lambda k, a=a: a[:, k, tok(t)]) for a in (hi, lo)]

            def natural(par, free, t, b):
                pe.wait_ge(unit_free, free)
                mm3(bank[b][:, 0:CW], tiles(xh, xl, t), weights(par, 0, CW), KT_N).then_inc(unit_done, 1)

            def transposed(par, free, n, s, b):
                pe.wait_ge(unit_free, free)
                mm3(bank[b][:, 0:HALF], weights(par, n * P, P), halves(xh, xl, s), KT_N).then_inc(unit_done, 1)

            pe.wait_ge(con_in, 16)
            pe.wait_ge(x_in, 32)
            for k in range(KT_N):
                for t in range(QBLK):
                    last = turn(bank[k][:, t * P:(t + 1) * P], xn[:, t, k * P:(k + 1) * P])
                last.then_inc(xt_done, 1)
            pe.wait_ge(xh_done, 1)
            pe.wait_ge(xl_done, 1)
            for k in range(KT_N):
                last = turn(bank[0][:, k * NS:(k + 1) * NS], xn[0:NS, QBLK, k * P:(k + 1) * P])
            last.then_inc(xt_done, 1)
            pe.wait_ge(xh_done, KT_N + 1)
            pe.wait_ge(xl_done, KT_N + 1)

            def attention_head(h):
                def unit(u):
                    return h * A_UNITS + (u + 3 if u == ZR_UNIT else u + 2)

                def group_free(n):
                    pe.wait_ge(tg_free[n % 2], h * (A_TG // 2) + (n // 2 + 1))
                    return bank[6 + n % 2]

                def group_read(n):
                    pe.wait_ge(tg_free[n % 2], h * (A_TG // 2) + (n // 2 + 2))

                def key_blocks(bi):
                    return [(0, k) for k in range(max(0, bi - 1), bi + 1)] + [(g, k) for g in (1, 2) for k in range(bi + 1)]

                def group_of(bi):
                    return (4, 5, 7, 9)[bi]

                def scores(bi):
                    pe.wait_ge(score_free, h * QBLK + (bi + 1))
                    for g in range(G):
                        lo = max(0, bi - 1) * P if g == 0 else 0
                        n = (bi + 1) * P - lo
                        last = pe.matmul(bank[3 + g][:, 0:n], qt[:, g, bi * P:(bi + 1) * P], kt[:, g, lo:lo + n],
                                         start=True, stop=True)
                    last.then_inc(score_done, 1)

                def probs_by_key(bi, lo=0, hi=12):
                    if lo == 0:
                        pe.wait_ge(exp_done, h * QBLK + (bi + 1))
                    nb = len(key_blocks(bi))
                    for x in range(lo, min(nb, hi)):
                        n = group_of(bi) + x // 4
                        if x % 4 == 0:
                            b = group_free(n)
                        last = turn(b[:, (x % 4) * P:(x % 4 + 1) * P], sp_[:, bi % 2, x * P:(x + 1) * P])
                        if x % 4 == 3 or x == nb - 1:
                            last.then_inc(tg_done, 1)

                def output(bi):
                    pe.wait_ge(o_read, h * QBLK + (bi + 1))
                    blocks = key_blocks(bi)
                    for x, (g, k) in enumerate(blocks):
                        if x % 4 == 0:
                            group_read(group_of(bi) + x // 4)
                        last = pe.matmul(bank[2][:, 0:P], pt[:, bi % 2, x * P:(x + 1) * P],
                                         kv[:, k, (G + g) * DH:(G + g + 1) * DH], start=(x == 0), stop=(x == len(blocks) - 1))
                    last.then_inc(o_done, 1)

                for j in range(2):
                    chunk_ready(h * A_CH + j)
                    for t in range(TT):
                        natural(j % 2, unit(5 * j + t), t, unit_bank(5 * j + t))

                def query_unit(u):
                    transposed(0, unit(u), (u - 10) // 2, u % 2, unit_bank(u))

                def q2_za_unit(u):
                    transposed(1, unit(u), (u - 14) // 2, u % 2, unit_bank(u))

                def value_unit(u):
                    natural(0, unit(u), u - 18, unit_bank(u))

                def zr_unit(u):
                    transposed(1, unit(u), (u - ZR_UNIT) // 2, (u - ZR_UNIT) % 2, unit_bank(u))

                chunk_ready(h * A_CH + 2)
                query_unit(10)
                pe.wait_ge(unit_free, h * A_UNITS + (3 + 10))
                for g in range(2):
                    b = group_free(g)
                    for t in range(QBLK):
                        last = turn(b[:, t * P:(t + 1) * P], kv[:, t, g * DH:(g + 1) * DH])
                    last.then_inc(tg_done, 1)
                for u in (11, 12, 13):
                    query_unit(u)
                b = group_free(2)
                for t in range(QBLK):
                    last = turn(b[:, t * P:(t + 1) * P], kv[:, t, 2 * DH:3 * DH])
                last.then_inc(tg_done, 1)
                b = group_free(3)
                settle(pe)
                for g in range(G):
                    last = turn(b[:, g * NS:(g + 1) * NS], ks[:, g * DH:(g + 1) * DH])
                last.then_inc(tg_done, 1)
                chunk_ready(h * A_CH + 3)
                for u in (14, 15, 16):
                    q2_za_unit(u)
                group_read(2)
                group_read(3)
                pe.wait_ge(unit_free, h * A_UNITS + (3 + 16))
                scores(0)
                q2_za_unit(17)
                scores(1)
                chunk_ready(h * A_CH + 4)
                value_unit(18)
                value_unit(19)
                probs_by_key(0)
                value_unit(20)
                scores(2)
                value_unit(21)
                probs_by_key(1)
                value_unit(22)
                scores(3)
                chunk_ready(h * A_CH + 5)
                zr_unit(23)
                pe.wait_ge(unit_free, h * A_UNITS + (3 + 23))
                output(0)
                probs_by_key(2)
                output(1)
                zr_unit(24)
                probs_by_key(3, 0, 8)
                output(2)
                probs_by_key(3, 8)
                zr_unit(25)
                output(3)
                zr_unit(26)
                for n in range(2):
                    pe.wait_ge(o_read, h * QBLK + (2 * n + 3))
                    b = group_free(12 + n)
                    for x in range(2):
                        last = turn(b[:, x * P:(x + 1) * P], on[:, 2 * n + x, :])
                    last.then_inc(tg_done, 1)

            with pe.Fori(0, H) as h:
                attention_head(h)
            pe.wait_ge(unit_free, 3 + U_B)
            for b in range(2):
                pe.wait_ge(tg_free[b], TB_B + 1)
            pe.matmul(bank[7][:, 0:1], ident, ident[:, 0:1], start=True, stop=True).then_inc(a_end, 1)
            pe.wait_ge(a_end, 4)

            def retention_head(r):
                def unit(u):
                    return r * B_UNITS + (U_B + u + 2)

                def cached_scores(x):
                    def transpose_tile(j):
                        n = 13 * x + j
                        if j in (0, 5, 9):
                            pe.wait_ge(slot_in[(0, 5, 9).index(j)], r * 128 + (64 * x + 32))
                        pe.wait_ge(tg_free[n % 2], r * 13 + (TB_B + n // 2 + 1))
                        s, k = (0, j) if j < 5 else (1, j - 5) if j < 9 else (2, j - 9)
                        for h in range(H):
                            last = turn(bank[2 + n % 2][:, h * P:(h + 1) * P], cslot[s][:, k, h * DH:(h + 1) * DH])
                        last.then_inc(tg_done, 1)

                    def score_tile(j):
                        n = 13 * x + j
                        pe.wait_ge(tg_free[n % 2], r * 13 + (TB_B + n // 2 + 2))
                        g, m, block = (0, 0, 0) if j == 0 else (1, j - 1, 12) if j < 5 else (2, j - 5, 28)
                        for h in range(H):
                            o = (block + m * H + h) * ROWS
                            pe.matmul(bank[4][0:ROWS, g * P:(g + 1) * P], qm[:, o:o + ROWS], ckt[:, n % 2, h * P:(h + 1) * P],
                                      start=(m == 0 and h == 0), stop=(j in (0, 4, 12) and h == H - 1))

                    transpose_tile(0)
                    pe.wait_ge(co_read, r * 2 + (x + 1))
                    pe.wait_ge(qm_done, r * 2 + (x + 1))
                    settle(pe)
                    for j in range(13):
                        if j + 1 < 13:
                            transpose_tile(j + 1)
                        score_tile(j)
                    for g in range(G):
                        for h in range(H):
                            o = (g * H + h) * ROWS
                            last = pe.matmul(bank[5][0:ROWS, g * NS:(g + 1) * NS], qm[:, o:o + ROWS],
                                             ktn[:, (h * G + g) * NS:(h * G + g + 1) * NS], start=(h == 0), stop=(h == H - 1))
                    last.then_inc(cs_done, 1)

                def cached_probs(x):
                    pe.wait_ge(rows_exp, r * 2 + (x + 1))
                    settle(pe)
                    for g in range(G):
                        turn(bank[5][:, 192 + g * ROWS:192 + (g + 1) * ROWS], srow[:, g * P:(g + 1) * P])
                        last = turn(bank[5][0:NS, 288 + g * ROWS:288 + (g + 1) * ROWS],
                                    srow[:, 384 + g * NS:384 + (g + 1) * NS])
                    last.then_inc(cp_done, 1)

                def cached_output(x):
                    pe.wait_ge(cp_read, r * 2 + (x + 1))
                    for j in range(13):
                        if j in (0, 5, 9):
                            pe.wait_ge(slot_in[(0, 5, 9).index(j)], r * 128 + (64 * x + 64))
                        s, k = (0, j) if j < 5 else (1, j - 5) if j < 9 else (2, j - 9)
                        last = pe.matmul(bank[4][0:ROWS, :], pm[:, j * ROWS:(j + 1) * ROWS], cslot[s][:, k, :],
                                         start=(j == 0), stop=False)
                        if j in (4, 8, 12):
                            last.then_inc(slot_free[(4, 8, 12).index(j)], 1)
                    new = vn[:, :].rearrange("p (h g e) -> p h g e", g=G, e=DH)
                    for g in range(G):
                        last = pe.matmul(bank[4][0:ROWS, :], pn[:, g * ROWS:(g + 1) * ROWS], new[:, :, g, :],
                                         start=False, stop=(g == G - 1))
                    last.then_inc(co_done, 1)

                def cached_turn(x):
                    pe.wait_ge(co_scaled, r * 2 + (x + 1))
                    settle(pe)
                    for h in range(H):
                        last = turn(bank[5][:, 384 + h * ROWS:384 + (h + 1) * ROWS], srow[:, h * DH:(h + 1) * DH])
                    last.then_inc(ct_done, 1)

                def group(n):
                    pe.wait_ge(rt_free[n % 2], r * 9 + (n // 2 + 1))
                    return bank[6 + n % 2]

                def group_read(n):
                    pe.wait_ge(rt_free[n % 2], r * 9 + (n // 2 + 2))

                def blocks(f, n=QBLK):
                    for t in range(n):
                        last = f(t, slice(t * P, (t + 1) * P))
                    last.then_inc(rt_done, 1)

                chunk_ready(r * B_CH + C0_B)
                for t in range(TT):
                    natural(0, unit(t), t, t % 2)
                cached_scores(0)
                chunk_ready(r * B_CH + (C0_B + 1))
                for t in range(3):
                    natural(1, unit(5 + t), t, (5 + t) % 2)
                pe.wait_ge(rot_done, r + 1)
                b = group(0)
                blocks(lambda t, c: turn(b[:, c], rot[:, t, 0:RK]))
                b = group(1)
                blocks(lambda t, c: turn(b[:, c], rot[:, t, RK:2 * RK]))
                b = group(2)
                settle(pe)
                turn(b[:, 0:NS], rot[0:NS, QBLK, 0:RK])
                turn(b[:, NS:2 * NS], rot[0:NS, QBLK, RK:2 * RK]).then_inc(rt_done, 1)
                cached_probs(0)
                for t in range(3, TT):
                    natural(1, unit(5 + t), t, (5 + t) % 2)
                group_read(0)
                group_read(1)
                b = group(3)
                blocks(lambda t, c: pe.matmul(b[:, c], krt[:, c], qrt[:, c], start=True, stop=True))
                pe.wait_ge(kd_done, r + 2)
                pe.wait_ge(unit_free, r * B_UNITS + (3 + U_B + 10))
                for n in range(2):
                    b = group(4 + n)
                    for t in range(2):
                        last = pe.matmul(b[:, t * RV:(t + 1) * RV], kd[:, 2 * n + t, :], vr[:, 2 * n + t, :],
                                         start=True, stop=True)
                    last.then_inc(rt_done, 1)
                group_read(2)
                b = group(6)
                pe.matmul(b[0:NS, 0:NS], qkts[:, NS:2 * NS], qkts[:, 0:NS], start=True, stop=True).then_inc(rt_done, 1)
                cached_output(0)
                group_read(3)
                group_read(4)
                for n in range(2):
                    b = group(7 + n)
                    if n == 0:
                        group_read(5)
                    for t in range(2 * n, 2 * n + 2):
                        o = b[:, (t % 2) * RV:(t % 2 + 1) * RV]
                        last = pe.matmul(o, krt[:, t * P:(t + 1) * P], vr[:, t, :], start=True, stop=(t == 0))
                        if t:
                            last = pe.matmul(o, qdt[:, t * P:(t + 1) * P], schain[:, t - 1, :], start=False, stop=True)
                    last.then_inc(rt_done, 1)
                group_read(6)
                pe.wait_ge(st_in, r * 16 + 16)
                b = group(9)
                settle(pe)
                pe.matmul(b[0:NS, 0:RV], atts[:, :], vr[0:NS, QBLK, :], start=True, stop=False)
                for n in range(DEC_B):
                    last = pe.matmul(b[0:NS, 0:RV], qdm[:, n * NS:(n + 1) * NS], st[:, n, :],
                                     start=False, stop=(n == DEC_B - 1))
                last.then_inc(rt_done, 1)
                cached_turn(0)
                pe.wait_ge(km_done, r + 1)
                for n in range(4):
                    b = group(10 + n)
                    for x in range(2):
                        o = (2 * n + x) * RK
                        last = pe.matmul(b[:, x * RV:(x + 1) * RV], km[:, o:o + RK], vr[0:NS, QBLK, :],
                                         start=True, stop=True)
                    last.then_inc(rt_done, 1)
                cached_scores(1)
                pe.wait_ge(normed, r + 1)
                for e in range(2):
                    b = group(14 + e)
                    blocks(lambda t, c: turn(b[:, c], qk[:, t, e * P:(e + 1) * P]))
                for e in range(2):
                    b = group(16 + e)
                    settle(pe)
                    turn(b[:, 0:NS], qk[0:NS, QBLK, e * P:(e + 1) * P]).then_inc(rt_done, 1)
                cached_probs(1)
                cached_output(1)
                cached_turn(1)

            with pe.Fori(0, RH) as r:
                retention_head(r)
            for b in range(2):
                pe.wait_ge(rt_free[b], RH * 9 + 1)
            pe.wait_ge(co_read, 2 * RH + 1)
            pe.matmul(bank[0][:, 0:1], ident, ident[:, 0:1], start=True, stop=True).then_inc(b_end, 1)
            pe.wait_ge(b_end, 4)

            def feature_tile(f):
                chunk_ready(f * C_CH + C0_C)
                for u in range(4):
                    pe.wait_ge(gt_free, f * 4 + (u + 1))
                    mm3(bank[u][:, 0:HALF], weights(0, (u // 2) * P, P), halves(xh, xl, u % 2), KT_N).then_inc(gt_done, 1)
                chunk_ready(f * C_CH + (C0_C + 1))
                pe.wait_ge(split_h, 2)
                pe.wait_ge(split_l, 2)
                for u in range(4):
                    pe.wait_ge(br_free, f * 4 + (u + 1))
                    hi, lo, k0, n = (oah, oal, 0, H) if u < 2 else (ybh, ybl, H, 2 * RH)
                    w = [(lambda k, a=a: a[1][:, (k + k0) // 6 * HW + (k + k0) % 6 * P:][:, 0:P]) for a in (wh, wl)]
                    mm3(bank[4 + u][:, 0:HALF], w, halves(hi, lo, u % 2), n).then_inc(br_done, 1)

            with pe.Fori(0, KT_N) as f:
                feature_tile(f)
            pe.wait_ge(gt_free, 4 + 4 * KT_N)
            pe.wait_ge(br_free, 4 + 4 * KT_N)
            pe.wait_ge(ul_done, KT_N)
            for n in range(4):
                chunk_ready(C0_O + n)
                for t in range(TT):
                    v = n * TT + t
                    if v >= 8:
                        pe.wait_ge(ou_free, v - 7)
                    mm3(bank[v % 8][:, 0:CW], tiles(uh, ul, t), weights(n % 2, 0, CW), KT_N).then_inc(ou_done, 1)

        @block.scalar
        def _(act):
            def high(c, par, used, n=HW):
                for s in range(2):
                    act.wait_ge(w_in_s[s], c * 32 + 32)
                    if s == 0:
                        used()
                    act.activation(wh[par][:, s * HW:s * HW + n], wraw[s][:, 0:n], ACT.Copy).then_inc(w_high, 1)

            act.wait_ge(credits, 1)
            high(0, 0, lambda: None)
            for k in range(KT_N + 1):
                act.wait_ge(xt_done, k + 1)
                if k < KT_N:
                    act.activation(xh[:, k, NS:NTOK], bank[k][:, :], ACT.Copy).then_inc(xh_done, 1)
                else:
                    act.activation(xh[:, :, 0:NS], bank[0][:, :].rearrange("p (k n) -> p k n", n=NS), ACT.Copy)\
                        .then_inc(xh_done, 1)

            def attention_head(h):
                def group(n, out, width):
                    act.wait_ge(tg_done, h * A_TG + (TD + n + 1))
                    act.activation(out, bank[6 + n % 2][:, 0:width], ACT.Copy).then_inc(tg_free[n % 2], 1)

                def sigmoid(u, n):
                    act.wait_ge(unit_done, h * A_UNITS + (UD + u + 1))
                    act.wait_ge(gate_free, h * 6 + (n + 1))
                    act.activation(sg[:, n % 2, :], bank[unit_bank(u)][:, 0:HALF], ACT.Sigmoid).then_inc(gate_sig, 1)

                def exponential(bi):
                    act.wait_ge(max_done, h * QBLK + (bi + 1))
                    n = min(2, bi + 1) * P + 2 * (bi + 1) * P
                    act.activation(sp_[:, bi % 2, 0:n], sp_[:, bi % 2, 0:n], ACT.Exp, bias=nmax[:, bi:bi + 1],
                                   accum_out=rsum[:, bi:bi + 1]).then_inc(exp_done, 1)

                def probs(bi, n):
                    nb = min(2, bi + 1) + 2 * (bi + 1)
                    x = (n - (4, 5, 7, 9)[bi]) * 4
                    w = min(4, nb - x) * P
                    group(n, pt[:, bi % 2, x * P:x * P + w], w)

                def next_high(j):
                    at = (-4, 0, 5, 10, 14, 18)[(j + 1) % 6]
                    more = 27 if j == 5 else 0
                    high(h * A_CH + (j + 1), (j + 1) % 2,
                         lambda: act.wait_ge(unit_done, h * A_UNITS + (UD + at + more)))

                next_high(0)
                next_high(1)
                group(0, kt[:, 0, :], SEQ)
                next_high(2)
                group(2, kt[:, 2, :], SEQ)
                next_high(3)
                sigmoid(16, 0)
                sigmoid(17, 1)
                exponential(0)
                exponential(1)
                next_high(4)
                probs(0, 4)
                exponential(2)
                probs(1, 6)
                next_high(5)
                sigmoid(23, 2)
                probs(2, 8)
                exponential(3)
                sigmoid(24, 3)
                probs(3, 10)
                sigmoid(25, 4)
                sigmoid(26, 5)

            with act.Fori(0, H) as h:
                attention_head(h)
            act.sem_inc(a_end, 1)

            def retention_head(r):
                def used_b(n):
                    return lambda: act.wait_ge(unit_done, r * B_UNITS + (UD + U_B + n))

                def keys(x):
                    for n in range(13 * x, 13 * x + 13):
                        if n % 2 == 0:
                            act.wait_ge(tg_done, r * B_TG + (TG_B + n + 1))
                            act.activation(ckt[:, 0, :], bank[2][:, :], ACT.Copy).then_inc(tg_free[0], 1)

                def rows(x):
                    act.wait_ge(rows_max, r * 2 + (x + 1))
                    act.activation(srow[:, :], srow[:, :], ACT.Exp, bias=smx[:, 0:1], accum_out=smx[:, 1:2])\
                        .then_inc(rows_exp, 1)

                def group(n, out, in_):
                    act.wait_ge(rt_done, r * 18 + (n + 1))
                    act.activation(out, in_, ACT.Copy).then_inc(rt_free[n % 2], 1)

                high(r * B_CH + (C0_B + 1), 1, used_b(0))
                keys(0)
                rows(0)
                group(1, krt[:, :], bank[7][:, :])
                high(r * B_CH + (C0_B + 2), 0, used_b(6))
                group(7, qk[:, 0:2, :], bank[7][:, :].rearrange("p (t e) -> p t e", e=RV))
                group(8, qk[:, 2:4, :], bank[6][:, :].rearrange("p (t e) -> p t e", e=RV))
                keys(1)
                rows(1)

            act.wait_ge(a_end, 4)
            with act.Fori(0, RH) as r:
                retention_head(r)
            act.sem_inc(b_end, 1)
            act.wait_ge(b_end, 4)

            act.activation(oah[:, :, :].rearrange("p k n -> p (k n)"), oa[:, :], ACT.Copy).then_inc(split_h, 1)
            act.activation(ybh[:, :, :].rearrange("p k n -> p (k n)"), yb[:, :], ACT.Copy).then_inc(split_h, 1)
            act.wait_ge(split_l, 2)
            with act.Fori(0, KT_N) as f:
                high(f * C_CH + (C0_C + 1), 1, lambda: act.wait_ge(br_done, f * 4 + 1), 6 * P)
                act.wait_ge(u_done, f + 1)
                for u in range(4):
                    act.wait_ge(gt_done, f * 4 + (u + 1))
                    act.activation(sgc[:, u // 2, (u % 2) * HALF:(u % 2 + 1) * HALF], bank[u][:, 0:HALF], ACT.Sigmoid)\
                        .then_inc(gt_free, 1)
                high(f * C_CH + (C0_C + 2), 0, lambda: act.wait_ge(gt_done, f * 4 + 4))
                act.wait_ge(u_done, f + 2)
                act.activation(uh[:, bass.ds(f, 1), :].rearrange("p k n -> p (k n)"), uc[:, 0, :], ACT.Copy)\
                    .then_inc(uh_done, 1)
            high(C0_O + 1, 1, lambda: act.wait_ge(br_done, 1 + 4 * KT_N))
            high(C0_O + 2, 0, lambda: act.wait_ge(ou_done, TT))
            high(C0_O + 3, 1, lambda: act.wait_ge(ou_done, 2 * TT))
            for t in range(TT):
                m = P if t < QBLK else NS
                act.wait_ge(y_done, t + 1)
                dst = y_prompt[0, t * P:(t + 1) * P, :] if t < QBLK else y_sample.rearrange("b t d -> (b t) d")
                act.dma_start(dst, z[0:m, t, :]).then_inc(y_stored, 16)
            act.wait_ge(y_stored, 16 * TT)

        @block.vector
        def _(dve):
            own = Links(dve, dve_l)
            tt = dve.tensor_tensor

            def low(c, par, n=HW):
                for s in range(2):
                    dve.wait_ge(w_high, c * 2 + (s + 1))
                    tt(wl[par][:, s * HW:s * HW + n], wraw[s][:, 0:n], wh[par][:, s * HW:s * HW + n].bitcast(F32),
                       ALU.subtract).then_inc(w_low, 1)

            dve.wait_ge(credits, 1)
            low(0, 0)
            for k in range(KT_N + 1):
                dve.wait_ge(xh_done, k + 1)
                if k < KT_N:
                    tt(xl[:, k, NS:NTOK], bank[k][:, :], xh[:, k, NS:NTOK].bitcast(F32), ALU.subtract).then_inc(xl_done, 1)
                else:
                    tt(xl[:, :, 0:NS], bank[0][:, :].rearrange("p (k n) -> p k n", n=NS), xh[:, :, 0:NS].bitcast(F32),
                       ALU.subtract).then_inc(xl_done, 1)
            dve.wait_ge(con_in, 16)
            dve.wait_ge(nd_in, 16)

            def attention_head(h):
                def unit(u):
                    dve.wait_ge(unit_done, h * A_UNITS + (UD + u + 1))
                    return bank[unit_bank(u)]

                def group(n):
                    dve.wait_ge(tg_done, h * A_TG + (TD + n + 1))
                    return bank[6 + n % 2]

                def queries(u, g, s):
                    b = unit(u)
                    if s == 0:
                        dve.tensor_scalar(qts[:, bass.ds(h * (G * NS) + g * NS, NS)], b[:, 0:NS], SCALE, None, ALU.mult)
                        dve.tensor_scalar(qt[:, g, 0:HALF - NS], b[:, NS:HALF], SCALE, None, ALU.mult).then_inc(unit_free, 1)
                    else:
                        dve.tensor_scalar(qt[:, g, HALF - NS:SEQ], b[:, 0:HALF], SCALE, None, ALU.mult).then_inc(unit_free, 1)

                def silu(u, n, out):
                    b = unit(u)
                    dve.wait_ge(gate_sig, h * 6 + (n + 1))
                    tt(out, b[:, 0:HALF], sg[:, n % 2, :], ALU.mult).then_inc(unit_free, 1)
                    dve.wait_ge(unit_free, h * A_UNITS + (3 + u + 1))
                    dve.sem_inc(gate_free, 1)

                def keys_values(u, t, lo):
                    b = unit(u)
                    if t < QBLK:
                        dve.tensor_copy(kv[:, t, lo:lo + CW], b[:, 0:CW]).then_inc(unit_free, 1)
                        return
                    nk = max(0, min(CW, G * DH - lo))
                    if nk:
                        i = dve.tensor_copy(ks[:, lo:lo + nk], b[0:NS, 0:nk])
                    if nk < CW:
                        i = dve.tensor_copy(vn[:, bass.ds(h * (G * DH) + (lo + nk - G * DH), CW - nk)], b[0:NS, nk:CW])
                    i.then_inc(unit_free, 1)

                def softmax(bi):
                    dve.wait_ge(score_done, h * QBLK + (bi + 1))
                    dve.wait_ge(tg_done, h * A_TG + (TD + (-5, -2, 5, 7)[bi]))
                    o = 0
                    for g in range(G):
                        n = (min(2, bi + 1) if g == 0 else bi + 1) * P
                        end = ND_O[g] + ND_W[g]
                        i = dve.scalar_tensor_tensor(
                            out=sp_[:, bi % 2, o:o + n], in0=nd[:, end - n:end],
                            scalar=const("slopes")[:, bass.ds(h * G + g, 1)], in1=bank[3 + g][:, 0:n],
                            op0=ALU.mult, op1=ALU.add)
                        o += n
                    i.then_inc(score_free, 1)
                    dve.wait_ge(score_free, h * QBLK + (bi + 2))
                    dve.tensor_reduce(nmax[:, bi:bi + 1], sp_[:, bi % 2, 0:o], AX.X, ALU.max, negate=True)\
                        .then_inc(max_done, 1)

                def probs(bi, n):
                    nb = min(2, bi + 1) + 2 * (bi + 1)
                    x = (n - (4, 5, 7, 9)[bi]) * 4
                    w = min(4, nb - x) * P
                    b = group(n)
                    dve.tensor_copy(pt[:, bi % 2, x * P:x * P + w], b[:, 0:w]).then_inc(tg_free[n % 2], 1)

                def output(bi):
                    dve.wait_ge(exp_done, h * QBLK + (bi + 1))
                    own.after(dve.reciprocal(rinv[:, bi:bi + 1], rsum[:, bi:bi + 1]))
                    dve.wait_ge(o_done, h * QBLK + (bi + 1))
                    dve.tensor_scalar(on[:, bi, :], bank[2][:, 0:P], rinv[:, bi:bi + 1], None, ALU.mult)\
                        .then_inc(o_read, 1)

                c = h * A_CH
                dve.wait_ge(kv_out, h + 1)
                for j in range(2):
                    low(c + (j + 1), (j + 1) % 2)
                    for t in range(TT):
                        keys_values(5 * j + t, t, CW * j)
                queries(10, 0, 0)
                b = group(1)
                dve.tensor_copy(kt[:, 1, :], b[:, :]).then_inc(tg_free[1], 1)
                low(c + 3, 1)
                for u in range(1, 4):
                    queries(10 + u, u // 2, u % 2)
                b = group(3)
                dve.tensor_copy(ktn[:, bass.ds(h * (G * NS), G * NS)], b[:, 0:G * NS]).then_inc(tg_free[1], 1)
                low(c + 4, 0)
                queries(14, 2, 0)
                queries(15, 2, 1)

                def za(n):
                    silu(16 + n, n, oa[:, bass.ds(h * NTOK + n * HALF, HALF)])

                def zr(n):
                    silu(23 + n, 2 + n, yb[:, bass.ds(h * (2 * NTOK) + n * HALF, HALF)])

                def values(u):
                    keys_values(u, u - 18, 2 * CW)

                za(0)
                softmax(0)
                za(1)
                softmax(1)
                values(18)
                values(19)
                low(c + 5, 1)
                values(20)
                softmax(2)
                values(21)
                probs(1, 5)
                values(22)
                softmax(3)
                zr(0)
                output(0)
                probs(2, 7)
                output(1)
                low(c + 6, 0)
                zr(1)
                probs(3, 9)
                output(2)
                probs(3, 11)
                zr(2)
                output(3)
                zr(3)
                for n in range(2):
                    b = group(12 + n)
                    o = oa[:, bass.ds(h * NTOK + (NS + 2 * n * P), 2 * P)]
                    tt(o, b[:, 0:2 * P], o, ALU.mult).then_inc(tg_free[n % 2], 1)

            with dve.Fori(0, H) as h:
                own.enter(h, 4)
                attention_head(h)
            own.leave(H)
            dve.wait_ge(tg_free[1], TB_B + 1)
            dve.sem_inc(a_end, 1)
            dve.wait_ge(a_end, 4)
            dve.wait_ge(gn_in, 16)
            dve.wait_ge(kd_done, 1)

            oav = oa[:, :].rearrange("p (h n) -> p h n", n=NTOK)

            def retention_head(r):
                def unit(u):
                    dve.wait_ge(unit_done, r * B_UNITS + (UD + U_B + u + 1))
                    return bank[u % 2]

                def group(n):
                    dve.wait_ge(rt_done, r * 18 + (n + 1))
                    return bank[6 + n % 2]

                def keys(x):
                    for n in range(13 * x, 13 * x + 13):
                        if n % 2:
                            dve.wait_ge(tg_done, r * B_TG + (TG_B + n + 1))
                            dve.tensor_copy(ckt[:, 1, :], bank[3][:, :]).then_inc(tg_free[1], 1)

                def queries(x):
                    dve.wait_ge(cs_done, r * 2 + (x + 1))
                    dve.wait_ge(credits, 1)
                    src = qts[:, :].rearrange("p (h g b q) -> p g h b q", g=G, b=DEC_B, q=DEC_T)

                    def of(g):
                        return src[:, g, :, bass.ds(r * 2 + x, 1), :].rearrange("p h b q -> p h (b q)")

                    def placed(o, *dims):
                        a = qm[:, o:o + 1]
                        return bass.AP(tensor=a.tensor, offset=a.offset, ap=[a.ap[0], *[list(d) for d in dims]])

                    for g in range(G):
                        dve.tensor_copy(placed(g * 4 * ROWS, (ROWS + DEC_T, H), (1, DEC_T)), of(g))
                    for e in range(2):
                        dve.tensor_copy(placed(12 * ROWS + 4 * e, (4 * ROWS + 1, 4), (ROWS + DEC_T, H)),
                                        of(1)[:, :, 4 * e:4 * e + 4].rearrange("p h j -> p j h"))
                    dve.tensor_copy(placed(28 * ROWS, (4 * ROWS + 1, DEC_T), (ROWS + DEC_T, H)),
                                    of(2).rearrange("p h j -> p j h")).then_inc(qm_done, 1)

                def rows(x):
                    dve.wait_ge(cs_done, r * 2 + (x + 2))
                    settle(dve)
                    tt(srow[:, 0:384], bank[4][0:ROWS, 0:384], const("biasc", ROWS), ALU.add)
                    bn = const("biasn", ROWS).rearrange("p (g n) -> p g n", g=G)[:, :, bass.ds(r * -16 + (56 - 8 * x), NS)]
                    own.after(tt(srow[:, 384:576].rearrange("p (g n) -> p g n", g=G),
                                 bank[5][0:ROWS, 0:G * NS].rearrange("p (g n) -> p g n", g=G), bn, ALU.add))
                    dve.tensor_reduce(smx[:, 0:1], srow[:, :], AX.X, ALU.max, negate=True).then_inc(rows_max, 1)

                def probs(x):
                    dve.wait_ge(cp_done, r * 2 + (x + 1))

                    def at(a, o, *dims):
                        a = a[:, o:o + 1]
                        return bass.AP(tensor=a.tensor, offset=a.offset, ap=[a.ap[0], *[list(d) for d in dims]])

                    dve.tensor_copy(pm[:, 0:ROWS], bank[5][:, 192:192 + ROWS])
                    dve.tensor_copy(at(pm, ROWS, (ROWS + 1, 4), (4, 2 * H)), at(bank[5], 224, (1, 4), (4, 2 * H)))
                    dve.tensor_copy(at(pm, 5 * ROWS, (ROWS + 1, DEC_T), (DEC_T, H)), at(bank[5], 256, (1, DEC_T), (DEC_T, H)))
                    dve.tensor_copy(pn[:, :], bank[5][0:NS, 288:384]).then_inc(cp_read, 1)

                def scale(x):
                    dve.wait_ge(rows_exp, r * 2 + (x + 1))
                    own.after(dve.reciprocal(smx[:, 2:3], smx[:, 1:2]))
                    dve.wait_ge(co_done, r * 2 + (x + 1))
                    dve.tensor_scalar(srow[:, 0:512], bank[4][0:ROWS, :], smx[:, 2:3], None, ALU.mult)\
                        .then_inc(co_scaled, 1)

                def output(x):
                    dve.wait_ge(ct_done, r * 2 + (x + 1))
                    o = oav[:, :, bass.ds(r * 16 + 8 * x, DEC_T)]
                    b = bank[5][:, 384:385]
                    b = bass.AP(tensor=b.tensor, offset=b.offset, ap=[b.ap[0], [ROWS + DEC_T, H], [1, DEC_T]])
                    tt(o, b, o, ALU.mult).then_inc(co_read, 1)

                def values(t):
                    b = unit(5 + t)
                    m = P if t < QBLK else NS
                    dve.tensor_copy(vr[0:m, t, :], b[0:m, 0:RV]).then_inc(unit_free, 1)

                queries(0)
                low(r * B_CH + (C0_B + 1), 1)
                for t in range(TT):
                    b = unit(t)
                    m = P if t < QBLK else NS
                    dve.tensor_copy(qk[0:m, t, :], b[0:m, 0:2 * RK]).then_inc(unit_free, 1)
                keys(0)
                rows(0)
                for t in range(3):
                    values(t)
                b = group(0)
                dve.tensor_copy(qrt[:, :], b[:, :])
                qdec = const("qdec").rearrange("p (r a n) -> p r a n", a=1, n=P)[:, bass.ds(r, 1), :, :]
                tt(qdt[:, :].rearrange("p (t n) -> p t n", n=P), b[:, :].rearrange("p (t n) -> p t n", n=P),
                   qdec.rearrange("p r a n -> p (r a) n").to_broadcast([P, QBLK, P]), ALU.mult).then_inc(rt_free[0], 1)
                b = group(2)
                dve.tensor_copy(qkts[:, :], b[:, 0:2 * NS])
                diag = qdm[:, 0:DEC_B * NS]
                diag = bass.AP(tensor=diag.tensor, offset=diag.offset, ap=[diag.ap[0], [NS + DEC_T, DEC_B], [1, DEC_T]])
                tt(diag, b[:, 0:NS].rearrange("p (b q) -> p b q", q=DEC_T),
                   const("qdecs")[:, bass.ds(r * NS, NS)].rearrange("p (b q) -> p b q", q=DEC_T), ALU.mult)\
                    .then_inc(rt_free[0], 1)
                probs(0)
                queries(1)
                values(3)
                values(4)
                b = group(3)
                dmat = const("dmat").rearrange("p (r n) -> p r n", n=P)[:, bass.ds(r, 1), :].to_broadcast([P, QBLK, P])
                tt(krt[:, :].rearrange("p (t n) -> p t n", n=P), b[:, :].rearrange("p (t n) -> p t n", n=P), dmat,
                   ALU.mult).then_inc(rt_free[1], 1)
                decay = const("cdec")[:, bass.ds(r * 2, 1)]
                dve.wait_ge(states_out, r + 1)
                b = group(4)
                own.after(dve.tensor_copy(schain[:, 0, :], b[:, 0:RV]))
                dve.scalar_tensor_tensor(out=schain[:, 1, :], in0=schain[:, 0, :], scalar=decay, in1=b[:, RV:2 * RV],
                                         op0=ALU.mult, op1=ALU.add).then_inc(rt_free[0], 1)
                dve.wait_ge(rt_free[0], r * 9 + 4)
                b = group(5)
                own.after(dve.scalar_tensor_tensor(out=schain[:, 2, :], in0=schain[:, 1, :], scalar=decay,
                                                   in1=b[:, 0:RV], op0=ALU.mult, op1=ALU.add))
                dve.scalar_tensor_tensor(out=schain[:, 3, :], in0=schain[:, 2, :], scalar=decay,
                                         in1=b[:, RV:2 * RV], op0=ALU.mult, op1=ALU.add).then_inc(rt_free[1], 1)
                b = group(6)
                tt(atts[:, :], b[0:NS, 0:NS], const("dmats", NS)[:, bass.ds(r * NS, NS)], ALU.mult).then_inc(rt_free[0], 1)
                scale(0)
                low(r * B_CH + (C0_B + 2), 0)
                b = group(9)
                dve.tensor_copy(qk[0:NS, QBLK, :], b[0:NS, 0:RV]).then_inc(rt_free[1], 1)
                dve.wait_ge(rt_free[1], r * 9 + 6)
                dve.wait_ge(rt_free[0], r * 9 + 6)
                for t in range(TT):
                    m = P if t < QBLK else NS
                    i = dve.bn_stats(bst[0:m, t, :], qk[0:m, t, :])
                own.after(i)
                settle(dve)
                for t in range(TT):
                    m = P if t < QBLK else NS
                    i = dve.bn_aggr(bmv[0:m, t, :], bst[0:m, t, :])
                i.then_inc(var_done, 1)
                output(0)
                decay8 = const("cdec")[:, bass.ds(r * 2 + 1, 1)]
                for n in range(4):
                    b = group(10 + n)
                    s = st[:, 2 * n:2 * n + 2, :]
                    dve.scalar_tensor_tensor(out=s, in0=s, scalar=decay8,
                                             in1=b[:, :].rearrange("p (b e) -> p b e", e=RV), op0=ALU.mult,
                                             op1=ALU.add).then_inc(rt_free[n % 2], 1)
                dve.wait_ge(rstd_done, r + 1)
                for t in range(TT):
                    m = P if t < QBLK else NS
                    i = dve.tensor_scalar(qk[0:m, t, :], qk[0:m, t, :], bmv[0:m, t, 0:1], rstd[0:m, t:t + 1],
                                          ALU.subtract, ALU.mult)
                i.then_inc(normed, 1)
                keys(1)
                rows(1)
                for n in range(4):
                    b = group(14 + n)
                    e, lo, w = n % 2, (NS if n < 2 else 0), (SEQ if n < 2 else NS)
                    o = yb[:, bass.ds(r * (2 * NTOK) + (e * NTOK + lo), w)]
                    dve.scalar_tensor_tensor(out=o, in0=b[:, 0:w], scalar=gn[:, bass.ds(r * 2 + e, 1)], in1=o,
                                             op0=ALU.mult, op1=ALU.mult).then_inc(rt_free[n % 2], 1)
                probs(1)
                scale(1)
                output(1)

            with dve.Fori(0, RH) as r:
                own.enter(r, 7)
                retention_head(r)
            own.leave(RH)
            dve.wait_ge(co_read, 2 * RH + 1)
            dve.sem_inc(b_end, 1)
            dve.wait_ge(b_end, 4)

            for n, (lo, src, hi) in enumerate(((oal, oa, oah), (ybl, yb, ybh))):
                dve.wait_ge(split_h, n + 1)
                tt(lo[:, :, :].rearrange("p k n -> p (k n)"), src[:, :],
                   hi[:, :, :].rearrange("p k n -> p (k n)").bitcast(F32), ALU.subtract).then_inc(split_l, 1)
            with dve.Fori(0, KT_N) as f:
                own.enter(f, 1)
                low(f * C_CH + (C0_C + 1), 1, 6 * P)
                dve.wait_ge(gt_free, f * 4 + 8)
                for u in range(4):
                    if u == 2:
                        low(f * C_CH + (C0_C + 2), 0)
                    dve.wait_ge(br_done, f * 4 + (u + 2))
                    s = slice((u % 2) * HALF, (u % 2 + 1) * HALF)
                    tt(uc[:, u // 2, s], bank[4 + u][:, 0:HALF], sgc[:, u // 2, s], ALU.mult).then_inc(br_free, 1)
                dve.wait_ge(br_free, f * 4 + 8)
                tt(uc[:, 0, :], uc[:, 0, :], uc[:, 1, :], ALU.add).then_inc(u_done, 1)
                dve.wait_ge(uh_done, f + 1)
                own.after(tt(ul[:, bass.ds(f, 1), :].rearrange("p k n -> p (k n)"), uc[:, 0, :],
                             uh[:, bass.ds(f, 1), :].rearrange("p k n -> p (k n)").bitcast(F32), ALU.subtract))
            own.leave(KT_N)
            dve.sem_inc(ul_done, KT_N)

            def normalise(t):
                m = P if t < QBLK else NS
                dve.wait_ge(zrstd_done, t + 1)
                own.after(dve.tensor_scalar(z[0:m, t, :], z[0:m, t, :], zmv[0:m, t, 0:1], zrs[0:m, t:t + 1],
                                            ALU.subtract, ALU.mult))
                own.after(tt(z[0:m, t, :], z[0:m, t, :], lng[0:m, :], ALU.mult))
                tt(z[0:m, t, :], z[0:m, t, :], lnb[0:m, :], ALU.add).then_inc(y_done, 1)

            dve.wait_ge(z_in, 32)
            dve.wait_ge(ln_in, 32)
            for n in range(4):
                if n < 3:
                    low(C0_O + n + 1, (n + 1) % 2)
                for t in range(TT):
                    v = n * TT + t
                    m = P if t < QBLK else NS
                    dve.wait_ge(ou_done, v + 1)
                    o = z[0:m, t, n * CW:(n + 1) * CW]
                    dve.scalar_tensor_tensor(out=o, in0=o, scalar=ALPHA, in1=bank[v % 8][0:m, 0:CW],
                                             op0=ALU.mult, op1=ALU.add).then_inc(ou_free, 1)
                    if n == 3:
                        dve.wait_ge(ou_free, v + 1)
                        for x in range(2):
                            i = dve.bn_stats(zst[0:m, t, 6 * x:6 * x + 6], z[0:m, t, 512 * x:512 * x + 512])
                        own.after(i)
                        dve.bn_aggr(zmv[0:m, t, :], zst[0:m, t, :]).then_inc(zvar_done, 1)
                        if t:
                            normalise(t - 1)
            normalise(TT - 1)


_INS = ["x_prompt", "x_sample", "cache_kv_w128", "cache_kv_w512", "cache_kv_w2048", "state_ret", "w_in", "w_pa",
        "w_pb", "w_o", "gn_g", "ln_g", "ln_b"]
_OUTS = ([(1, SEQ, D_MODEL), (DEC_B, DEC_T, D_MODEL)] + [(1, min(w, SEQ), 2, H, DH) for w, _ in GROUPS]
         + [(1, RH, RK, RV)] + [(DEC_B, w, 2, H, DH) for w, _ in GROUPS] + [(DEC_B, RH, RK, RV)])


def kernel(**inputs):
    import numpy as _np
    import concourse.bacc as _bacc
    from concourse import mybir as _mybir
    from concourse.bass_utils import run_bass_kernel_spmd as _run

    nc = _bacc.Bacc("TRN2", target_bir_lowering=False, num_devices=1)
    arrays = {name: _np.ascontiguousarray(inputs[name]) for name in _INS}
    arrays["gn_g"] = _np.ascontiguousarray(arrays["gn_g"].reshape(-1, P).T)
    arrays["consts"], arrays["dist_tab"] = shape_constants()
    arrays = {f"in_{name}_dram": a for name, a in arrays.items()}
    args = [nc.dram_tensor(name, a.shape, _mybir.dt.from_np(a.dtype), kind="ExternalInput").ap()
            for name, a in arrays.items()]
    for i, shape in enumerate(_OUTS):
        args.append(nc.dram_tensor(f"out_{i}_dram", shape, F32, kind="ExternalOutput").ap())
    bass_hybrid_step(nc, *args)
    r = _run(nc, [arrays], core_ids=[0])
    return tuple(r.results[0][f"out_{i}_dram"] for i in range(len(_OUTS)))
```

```python
import math
from contextlib import ExitStack

import numpy as np

import concourse.bass as bass
from concourse import mybir

F32 = mybir.dt.float32
F32R = mybir.dt.float32r
ALU = mybir.AluOpType
ACT = mybir.ActivationFunctionType
AX = mybir.AxisListType

P = 128
D_MODEL, D_IN = 1024, 10240
KT_N = D_MODEL // P
SEQ, DEC_B, DEC_T = 512, 8, 8
NS = DEC_B * DEC_T
NTOK = NS + SEQ
QBLK = SEQ // P
TT = QBLK + 1
HALF = NTOK // 2
GROUPS = ((128, 1), (512, 4), (2048, 16))
G, H, DH = 3, 4, 128
RH, RK, RV = 4, 128, 256
A_QKV, A_OUT = G * H * DH, H * DH
OFF_Q, OFF_K, OFF_V = 0, A_QKV, 2 * A_QKV
OFF_ZA = 3 * A_QKV
OFF_QR = OFF_ZA + A_OUT
OFF_KR = OFF_QR + RH * RK
OFF_VR = OFF_KR + RH * RK
OFF_ZR = OFF_VR + RH * RV
OFF_GA = OFF_ZR + RH * RV
OFF_GB = OFF_GA + D_MODEL
SCALE = DH ** -0.5
EPS = 1e-5
ALPHA = 2 ** 0.25
PAST = 2048
MASKED = -1e32
CW = 256
HW = KT_N * CW // 2
A_CH, B_CH, C_CH = 6, 2, 2
UD, TD = 5, 6
C0_B = H * A_CH
C0_C = C0_B + RH * B_CH
C0_O = C0_C + KT_N * C_CH
ZR_UNIT = 23
A_UNITS = 27
B_UNITS = 10
A_TG, B_TG = 14, 26
U_B = H * A_UNITS
TG_B = TD + H * A_TG
TB_B = H * A_TG // 2
A_COPY_B = 5
ROWS = H * DEC_T
BLK = 2 * ROWS
TILES = 13
SLOTS = ((0, 5), (5, 9), (9, 13))
ND_W = (256, 512, 512)
ND_O = (0, 256, 768)

_W = [("ident", P), ("slopes", 12), ("cos", TT * 64), ("sin", TT * 64), ("dmat", RH * P), ("small", 384), ("qdec", RH * P), ("kdec", RH * TT),
      ("cdec", RH * 2), ("bmask", DEC_B)]
COL, _o = {}, 0
for _n, _w in _W:
    COL[_n] = (_o, _w)
    _o += _w
NCONST = _o
SMALL = {"dmats": (0, RH * NS), "biasc": (64, 384), "biasn": (96, 360)}


def shape_constants():
    c = np.zeros((P, NCONST), np.float32)

    def put(name, a):
        o, w = COL[name if name in COL else "small"]
        p0, w = SMALL.get(name, (0, w))
        a = np.asarray(a, np.float32).reshape(a.shape[0], w)
        c[p0:p0 + a.shape[0], o:o + w] = a

    put("ident", np.eye(P))
    slope = 2.0 ** (-8.0 * np.arange(1, G * H + 1) / (G * H)).reshape(G, H)
    put("slopes", np.broadcast_to(slope.T.reshape(1, G * H), (P, G * H)))
    bc = np.zeros((H, DEC_T, G, P))
    bn = np.zeros((H, DEC_T, G, 120))
    m = np.arange(P)
    t = np.arange(120) - 56
    for q in range(DEC_T):
        idx = (m, 4 * m + q % 4, 16 * m + q)
        for g, (w, d) in enumerate(GROUPS):
            dist = w + q - idx[g]
            new = q - t
            ok = (t >= 0) & (new >= 0) & (new % d == 0)
            for h in range(H):
                bc[h, q, g] = np.where(dist <= w, -slope[g, h] * dist, MASKED)
                bn[h, q, g] = np.where(ok, -slope[g, h] * new, MASKED)
    put("biasc", bc.reshape(H * DEC_T, -1))
    put("biasn", bn.reshape(H * DEC_T, -1))
    f32 = np.float32
    frac = np.arange(64, dtype=f32) * (f32(1) / f32(63))
    inv = (f32(1) / (10000.0 ** frac.astype(np.float64)).astype(f32)).astype(f32)
    pos = np.zeros((P, TT), np.float32)
    for k in range(QBLK):
        pos[:, k] = k * P + np.arange(P)
    pos[:, QBLK] = PAST + np.arange(P) % DEC_T
    ang = (pos[:, :, None] * inv).astype(np.float32).astype(np.float64)
    put("cos", np.cos(ang))
    put("sin", np.sin(ang))
    lg = np.log1p(-np.exp2(-5.0 - np.arange(RH)))
    i = np.arange(P)
    diff = i[None, :] - i[:, None]
    ks = RK ** -0.5
    put("dmat", (np.where(diff >= 0, np.exp(np.maximum(diff, 0) * lg[:, None, None]), 0) * ks).transpose(1, 0, 2))
    j = np.arange(NS)
    ds = j[None, :] - j[:, None]
    same = (j[None, :] // DEC_T == j[:, None] // DEC_T) & (ds >= 0)
    put("dmats", (np.where(same, np.exp(np.maximum(ds, 0) * lg[:, None, None]), 0) * ks).transpose(1, 0, 2))
    put("qdec", np.broadcast_to(np.exp((i + 1) * lg[:, None]), (P, RH, P)))
    kd = np.zeros((P, RH, TT))
    for r in range(RH):
        kd[:, r, :QBLK] = (np.exp((P - 1.0 - i) * lg[r]) * ks)[:, None]
        kd[:, r, QBLK] = np.exp((DEC_T - 1.0 - i % DEC_T) * lg[r]) * ks
    put("kdec", kd)
    put("cdec", np.broadcast_to(np.stack([np.exp(P * lg), np.exp(DEC_T * lg)], 1), (P, RH, 2)))
    put("bmask", (i[:NS, None] // DEC_T == np.arange(DEC_B)[None]).astype(np.float32))
    nd = np.zeros((P, sum(ND_W)), np.float32)
    for g, (w, d) in enumerate(GROUPS):
        x = np.arange(ND_W[g]) - (ND_W[g] - P)
        dist = i[:, None] - x[None, :]
        ok = (dist >= 0) & (dist <= w) & (dist % d == 0)
        nd[:, ND_O[g]:ND_O[g] + ND_W[g]] = np.where(ok, -dist, MASKED)
    return c, nd


X_ORDER = [(0, 1), (1, 2), (None, 0), (2, 3), (3, 4), (4, 5), (5, 6), (6, 7), (7, 1)]


def unit_bank(u):
    return (u + (u >= ZR_UNIT)) % 2


class Links:

    def __init__(self, eng, sem):
        self.eng, self.sem, self.base, self.n, self.turn, self.per = eng, sem, 0, 0, None, 0

    def enter(self, turn, per):
        self.base, self.turn, self.per, self.n = self.base + self.n, turn, per, 0

    def leave(self, turns):
        assert self.n == self.per, f"links per turn: {self.n}, not {self.per}"
        self.base, self.turn, self.n = self.base + turns * self.per, None, 0

    def after(self, ins):
        ins.then_inc(self.sem, 1)
        self.n += 1
        v = self.base + self.n
        self.eng.wait_ge(self.sem, v if self.turn is None else self.turn * self.per + v)


def bass_hybrid_step(nc, x_prompt, x_sample, cache128, cache512, cache2048, state_ret, w_in, w_pa, w_pb, w_o,
                     gn_t, ln_g, ln_b, consts, dist_tab,
                     y_prompt, y_sample, kv128_p, kv512_p, kv2048_p, ret_p, kv128_s, kv512_s, kv2048_s, ret_s):
    caches = (cache128, cache512, cache2048)
    kv_p = (kv128_p, kv512_p, kv2048_p)
    kv_s = (kv128_s, kv512_s, kv2048_s)

    with ExitStack() as ctx:
        def sb(name, shape, dt=F32, scope=ctx):
            return scope.enter_context(nc.sbuf_tensor(name, shape, dt))

        def sem(name):
            return ctx.enter_context(nc.semaphore(name))

        bank = [ctx.enter_context(nc.psum_tensor(f"bank{b}", [P, 512], F32)) for b in range(8)]

        xh = sb("xh", [P, KT_N, NTOK], F32R)
        xl = sb("xl", [P, KT_N, NTOK], F32R)
        raw = sb("raw", [P, 2 * HW])
        wraw = [raw[:, s * HW:(s + 1) * HW] for s in range(2)]
        wh = [sb(f"wh{b}", [P, 2 * HW], F32R) for b in range(2)]
        wl = [sb(f"wl{b}", [P, 2 * HW], F32R) for b in range(2)]
        con = sb("con", [P, NCONST])
        gn = sb("gn", [P, RH * RV // P])

        def const(name, parts=P):
            o, w = COL[name if name in COL else "small"]
            p0, w = SMALL.get(name, (0, w))
            return con[p0:p0 + parts, o:o + w]

        ident = const("ident")
        scope_c = ExitStack()
        scope_ab = ExitStack()
        oa = sb("oa", [P, H * NTOK], F32, scope_ab)
        yb = sb("yb", [P, 2 * RH * NTOK], F32, scope_ab)
        qts = sb("qts", [P, H * G * NS], F32, scope_ab)
        ktn = sb("ktn", [P, H * G * NS], F32, scope_ab)
        vn = sb("vn", [NS, H * G * DH], F32, scope_ab)
        scope_x = ExitStack()
        xn = sb("xn", [P, TT, D_MODEL], F32, scope_x)
        scope_x.close()
        scope_a = ExitStack()
        kv = sb("kv", [P, QBLK, 2 * G * DH], F32, scope_a)
        ks = sb("ks", [NS, G * DH], F32, scope_a)
        kt = sb("kt", [P, G, SEQ], F32, scope_a)
        qt = sb("qt", [P, G, SEQ], F32, scope_a)
        sp_ = sb("scoresp", [P, 2, 1280], F32, scope_a)
        pt = sb("pt", [P, 2, 1280], F32, scope_a)
        on = sb("on", [P, QBLK, DH], F32, scope_a)
        sg = sb("sg", [P, 2, HALF], F32, scope_a)
        nd = sb("nd", [P, sum(ND_W)], F32, scope_a)
        nmax = sb("nmax", [P, QBLK], F32, scope_a)
        rsum = sb("rsum", [P, QBLK], F32, scope_a)
        rinv = sb("rinv", [P, QBLK], F32, scope_a)
        scope_a.close()
        scope_b = ExitStack()
        cslot = [sb(f"cslot{s}", [P, n, H * DH], F32, scope_b) for s, n in enumerate((5, 4, 4))]
        part_h = [sb(f"part_h{b}", [P, H * P], F32R, scope_b) for b in range(3)]
        part_l = [sb(f"part_l{b}", [P, H * P], F32R, scope_b) for b in range(3)]
        qk = sb("qk", [P, TT, 2 * RK], F32, scope_b)
        rot = sb("rot", [P, TT, 2 * RK], F32, scope_b)
        kd = sb("kd", [P, TT, RK], F32, scope_b)
        vr = sb("vr", [P, TT, RV], F32, scope_b)
        qrt = qk[:, 0:2, :].rearrange("p t e -> p (t e)")
        qkts = qk[:, 2, 0:2 * NS]
        qdt = sb("qdt", [P, SEQ], F32, scope_b)
        krt = sb("krt", [P, SEQ], F32, scope_b)
        qdm = sb("qdm", [P, DEC_B * NS], F32, scope_b)
        atts = sb("atts", [NS, NS], F32, scope_b)
        st = raw[:, :].rearrange("p (b e) -> p b e", e=RV)
        schain = sb("schain", [P, QBLK, RV], F32, scope_b)
        qm = sb("qm", [P, 44 * BLK], F32R, scope_b)
        srow = sb("srow", [ROWS, 576], F32, scope_b)
        smx = sb("smx", [ROWS, 4], F32, scope_b)
        pm = sb("pm", [P, TILES * BLK], F32R, scope_b)
        pn = sb("pn", [NS, G * BLK], F32, scope_b)
        bst = sb("bst", [P, TT, 6], F32, scope_b)
        bmv = sb("bmv", [P, TT, 2], F32, scope_b)
        rstd = sb("rstd", [P, TT], F32, scope_b)
        half = sb("half", [P, TT], F32, scope_b)
        scope_b.close()
        scope_ab.close()
        km = rot[0:NS].rearrange("p a b -> p (a b)")[:, 0:DEC_B * RK]
        uh = sb("uh", [P, KT_N, NTOK], F32R, scope_c)
        ul = sb("ul", [P, KT_N, NTOK], F32R, scope_c)
        ybh = sb("ybh", [P, 2 * RH, NTOK], F32R, scope_c)
        ybl = sb("ybl", [P, 2 * RH, NTOK], F32R, scope_c)
        oah = sb("oah", [P, H, NTOK], F32R, scope_c)
        oal = sb("oal", [P, H, NTOK], F32R, scope_c)
        sgc = sb("sgc", [P, 2, NTOK], F32, scope_c)
        uc = sb("uc", [P, 2, NTOK], F32, scope_c)
        scope_c.close()
        scope_d = ExitStack()
        sb("uh_", [P, KT_N, NTOK], F32, scope_d)
        sb("ul_", [P, KT_N, NTOK], F32, scope_d)
        z = sb("z", [P, TT, D_MODEL], F32, scope_d)
        lng = sb("lng", [P, D_MODEL], F32, scope_d)
        lnb = sb("lnb", [P, D_MODEL], F32, scope_d)
        zst = sb("zst", [P, TT, 12], F32, scope_d)
        zmv = sb("zmv", [P, TT, 2], F32, scope_d)
        zrs = sb("zrs", [P, TT], F32, scope_d)
        zhf = sb("zhf", [P, TT], F32, scope_d)
        scope_d.close()

        ident_in, con_in, nd_in, gn_in = sem("ident_in"), sem("con_in"), sem("nd_in"), sem("gn_in")
        x_in = [sem(f"x_in{s}") for s in range(3)]
        passed = sem("passed")
        credits = sem("credits")
        xt_done = sem("xt_done")
        xh_done = sem("xh_done")
        xl_done = sem("xl_done")
        w_in_s = [sem(f"w_in{s}") for s in range(2)]
        w_high = sem("w_high")
        w_low = sem("w_low")
        unit_done = sem("unit_done")
        unit_free = sem("unit_free")
        gate_sig = sem("gate_sig")
        gate_free = sem("gate_free")
        tg_done = sem("tg_done")
        tg_free = [sem(f"tg_free{b}") for b in range(2)]
        score_done = sem("score_done")
        score_free = sem("score_free")
        max_done = sem("max_done")
        exp_done = sem("exp_done")
        o_done = sem("o_done")
        o_read = sem("o_read")
        k_stored, v_stored = sem("k_stored"), sem("v_stored")
        kv_out = sem("kv_out")
        states_out = sem("states_out")
        a_end, b_end = sem("a_end"), sem("b_end")
        slot_in = [sem(f"slot_in{s}") for s in range(3)]
        part_high, part_low = sem("part_high"), sem("part_low")
        part_used = sem("part_used")
        qm_done = sem("qm_done")
        cs_done, rows_max, rows_exp = sem("cs_done"), sem("rows_max"), sem("rows_exp")
        rows_norm = sem("rows_norm")
        cp_done, cp_read = sem("cp_done"), sem("cp_read")
        co_done = sem("co_done")
        co_lows, co_sum = sem("co_lows"), sem("co_sum")
        ct_done, co_read = sem("ct_done"), sem("co_read")
        rot_done, kd_done, km_done = sem("rot_done"), sem("kd_done"), sem("km_done")
        rt_done = sem("rt_done")
        rt_free = [sem(f"rt_free{b}") for b in range(2)]
        st_in, st_stored, sc_stored = sem("st_in"), sem("st_stored"), sem("sc_stored")
        var_done, rstd_done, normed = sem("var_done"), sem("rstd_done"), sem("normed")
        split_h, split_l = sem("split_h"), sem("split_l")
        gt_done, gt_free = sem("gt_done"), sem("gt_free")
        br_done, br_free = sem("br_done"), sem("br_free")
        u_done, uh_done, ul_done = sem("u_done"), sem("uh_done"), sem("ul_done")
        z_in, ln_in = sem("z_in"), sem("ln_in")
        ou_done, ou_free = sem("ou_done"), sem("ou_free")
        zvar_done, zrstd_done, y_done = sem("zvar_done"), sem("zrstd_done"), sem("y_done")
        y_stored, copied = sem("y_stored"), sem("copied")
        dve_l, pool_l = sem("dve_l"), sem("pool_l")
        CREDIT = [(w_low, 2), (unit_done, 5), (unit_free, 3), (gate_free, 2), (tg_done, 6), (score_free, 1),
                  (o_read, 1), (cs_done, 1), (part_low, 26), (part_used, 1), (co_read, 1), (kv_out, 1), (states_out, 1),
                  (gt_free, 4), (br_free, 4), (br_done, 1), (u_done, 1),
                  *((x, 1) for x in (*tg_free, *rt_free))]

        block = ctx.enter_context(nc.Block())

        def settle(eng):
            eng.sem_inc(passed, 1)

        @block.sync
        def _(sp):
            def load_half(c, s, pieces):
                sp.wait_ge(w_low, c * 2 + s + 1)
                settle(sp)
                for dst, src in pieces:
                    sp.dma_start(dst, src).then_inc(w_in_s[s], 16 * (2 // len(pieces)))

            def columns(c, offs, width, which=(0, 1)):
                for s in which:
                    dst = wraw[s].rearrange("p (k n) -> p k n", n=CW)
                    src = w_in.rearrange("(k p) n -> p k n", p=P)[:, 4 * s:4 * s + 4, :]
                    if width == CW:
                        pieces = [(dst, src[:, :, bass.ds(offs[0], CW)])]
                    else:
                        pieces = [(dst[:, :, n * width:(n + 1) * width], src[:, :, bass.ds(offs[n], width)])
                                  for n in range(2)]
                    load_half(c, s, pieces)

            half_x = D_MODEL // 2
            for s in range(2):
                if s == 0:
                    sp.dma_start(con[:, 0:P], consts[:, 0:P]).then_inc(ident_in, 16)
                sp.dma_start(xn[:, 0:QBLK, s * half_x:(s + 1) * half_x],
                             x_prompt[0].rearrange("(t p) d -> p t d", p=P)[:, :, s * half_x:(s + 1) * half_x])\
                    .then_inc(x_in[s], 16)
                if s == 0:
                    sp.dma_start(xn[0:NS, QBLK, :], x_sample.rearrange("b t d -> (b t) d")).then_inc(x_in[2], 16)
                    sp.wait_ge(credits, 1)
                columns(0, (OFF_K, OFF_K + 512), DH, (s,))
            sp.dma_start(con[:, P:NCONST], consts[:, P:NCONST]).then_inc(con_in, 16)

            def rows(g, b, lo, n):
                w = GROUPS[g][0]
                src = caches[g][b].rearrange("s c h d -> s (c h d)")[DEC_T:w]
                dst = kv_s[g][b].rearrange("s c h d -> s (c h d)")[0:w - DEC_T]
                sp.dma_start(dst[bass.ds(lo, n), :], src[bass.ds(lo, n), :]).then_inc(copied, 16)

            def stage_a(h, last):
                cols = [(OFF_K + 1024, OFF_V), (OFF_Q, OFF_Q + 512), (OFF_Q + 1024, OFF_ZA), (OFF_V + 512, OFF_V + 1024)]
                for j, (a, b) in enumerate(cols):
                    columns(h * A_CH + (j + 1), (h * DH + a, h * DH + b), DH)
                    rows(2, j, h * 510, 510)
                columns(h * A_CH + 5, (h * RV + OFF_ZR,), CW)
                rows(2, 4, h * 510, 510)
                if last:
                    columns(C0_B, (OFF_QR, OFF_KR), RK)
                else:
                    columns(h * A_CH + 6, (h * DH + (DH + OFF_K), h * DH + (DH + OFF_K + 512)), DH)
                for b in range(A_COPY_B):
                    rows(1, b, h * 126, 126)
                    rows(0, b, h * 30, 30)

            with sp.Fori(0, H - 1) as h:
                stage_a(h, False)
            stage_a(H - 1, True)

            sp.dma_start(gn[:, :], gn_t).then_inc(gn_in, 16)

            def retention_chunk(c, r, which):
                if which == 0:
                    columns(c, (r * RK + OFF_QR, r * RK + OFF_KR), RK)
                else:
                    columns(c, (r * RV + OFF_VR,), CW)

            def load_tiles(b, which, slot, tiles, parts):
                views = [caches[g].rearrange("b (m d) c h e -> b m d c (h e)", d=GROUPS[g][1]) for g in range(G)]

                def pick(g, lo, k):
                    return views[g][bass.ds(b, 1), :, lo:lo + k, which, :].rearrange("b m d e -> m (b d) e")

                sp.wait_ge(part_low, b * 26 + parts)
                if tiles[0] == 0:
                    sp.dma_start(cslot[slot][:, 0:1, :], pick(0, 0, 1)).then_inc(slot_in[slot], 16)
                    sp.dma_start(cslot[slot][:, 1:5, :], pick(1, 0, 4)).then_inc(slot_in[slot], 16)
                else:
                    sp.dma_start(cslot[slot][:, 0:4, :], pick(2, tiles[0] - 5, 4)).then_inc(slot_in[slot], 32)

            def keys(b):
                for slot, tiles in enumerate(SLOTS):
                    load_tiles(b, 0, slot, tiles, TILES + tiles[1])

            def values(b):
                for slot, tiles in enumerate(SLOTS):
                    load_tiles(b, 1, slot, tiles, 2 * TILES + tiles[1])

            sp.wait_ge(a_end, 4)

            def gate_chunk(c, f):
                columns(c, (f * P + OFF_GA, f * P + OFF_GB), P)

            def stage_b(r, last):
                keys(r * 2)
                retention_chunk(r * B_CH + (C0_B + 1), r, 1)
                values(r * 2)
                sp.wait_ge(w_low, r * (2 * B_CH) + (2 * C0_B + 6))
                sp.dma_start(st[:, :, :], state_ret[:, bass.ds(r, 1), :, :].rearrange("b r d e -> d (b r) e"))\
                    .then_inc(st_in, 16)
                keys(r * 2 + 1)
                values(r * 2 + 1)
                sp.wait_ge(states_out, r + 2)
                if last:
                    gate_chunk(C0_C, 0)
                else:
                    retention_chunk(r * B_CH + (C0_B + 2), r + 1, 0)

            with sp.Fori(0, RH - 1) as r:
                stage_b(r, False)
            stage_b(RH - 1, True)
            def branch_chunk(c, f):
                pa = w_pa.rearrange("(k p) n -> p k n", p=P)[:, :, bass.ds(f * P, P)]
                pb = w_pb.rearrange("(k p) n -> p k n", p=P)[:, :, bass.ds(f * P, P)]
                d = [wraw[s][:, 0:6 * P].rearrange("p (k n) -> p k n", n=P) for s in range(2)]
                load_half(c, 0, [(d[0][:, 0:4, :], pa), (d[0][:, 4:6, :], pb[:, 0:2, :])])
                load_half(c, 1, [(d[1], pb[:, 2:8, :])])

            def out_chunk(c, n):
                src = w_o.rearrange("(k p) n -> p k n", p=P)
                for s in range(2):
                    dst = wraw[s][:, :].rearrange("p (k n) -> p k n", n=CW)
                    load_half(c, s, [(dst, src[:, 4 * s:4 * s + 4, n * CW:(n + 1) * CW])])

            def stage_c(f, last):
                branch_chunk(f * C_CH + (C0_C + 1), f)
                for b in range(A_COPY_B, DEC_B):
                    rows(2, b, f * 255, 255)
                if last:
                    out_chunk(C0_O, 0)
                else:
                    gate_chunk(f * C_CH + (C0_C + 2), f + 1)
                for b in range(A_COPY_B, DEC_B):
                    rows(1, b, f * 63, 63)
                    rows(0, b, f * 15, 15)

            with sp.Fori(0, KT_N - 1) as f:
                stage_c(f, False)
            stage_c(KT_N - 1, True)
            for n in range(1, 4):
                out_chunk(C0_O + n, n)
                if n == 1:
                    sp.wait_ge(br_free, 4 + 4 * KT_N)
                    sp.dma_start(z[:, 0:QBLK, :], x_prompt[0].rearrange("(t p) d -> p t d", p=P)).then_inc(z_in, 16)
                    sp.dma_start(z[0:NS, QBLK, :], x_sample.rearrange("b t d -> (b t) d")).then_inc(z_in, 16)
                    for dst, src in ((lng, ln_g), (lnb, ln_b)):
                        sp.dma_start(dst[:, :], src.rearrange("(a d) -> a d", a=1).to_broadcast([P, D_MODEL]))\
                            .then_inc(ln_in, 16)
            sp.wait_ge(copied, 16 * (H * (5 + 2 * A_COPY_B) + KT_N * 3 * (DEC_B - A_COPY_B)))

        @block.gpsimd
        def _(pool):
            own = Links(pool, pool_l)
            tt = pool.tensor_tensor
            for s, n in CREDIT:
                pool.sem_inc(s, n)
            pool.sem_inc(credits, 1)
            pool.dma_start(nd[:, :], dist_tab).then_inc(nd_in, 16)

            def store_kv(h, which):
                done = k_stored if which == 0 else v_stored
                for g in range(G):
                    w = GROUPS[g][0]
                    o = (which * G + g) * DH
                    lo = QBLK - 1 if g == 0 else 0
                    dst = kv_p[g][0].rearrange("(t p) c h d -> p t c h d", p=P)[:, :, which, bass.ds(h, 1), :]
                    pool.dma_start(dst.rearrange("p t h d -> p t (h d)"), kv[:, lo:QBLK, o:o + DH]).then_inc(done, 16)
                    dst = kv_s[g][:, w - DEC_T:w, which, bass.ds(h, 1), :].rearrange("b t h d -> b t (h d)")
                    src = ks[:, g * DH:(g + 1) * DH] if which == 0 else vn[:, bass.ds(h * (G * DH) + g * DH, DH)]
                    pool.dma_start(dst, src).then_inc(done, 16)

            with pool.Fori(0, H) as h:
                pool.wait_ge(unit_free, h * A_UNITS + (3 + 10))
                store_kv(h, 0)
                pool.wait_ge(unit_free, h * A_UNITS + (3 + 23))
                store_kv(h, 1)
                pool.wait_ge(k_stored, h * 96 + 96)
                pool.wait_ge(v_stored, h * 96 + 96)
                pool.sem_inc(kv_out, 1)
            pool.sem_inc(a_end, 1)
            pool.wait_ge(a_end, 4)
            own.after(pool.memset(qk[NS:P, QBLK, :], 0.0))
            own.after(pool.memset(half[:, :], -0.5))
            own.after(pool.memset(pn[:, :], 0.0))
            pool.memset(qdm[:, :], 0.0).then_inc(kd_done, 1)
            pool.wait_ge(kd_done, 1)
            pool.wait_ge(con_in, 16)

            x1, x2 = (qk[:, :, :].rearrange("p t (c e) -> p t c e", c=2)[:, :, :, 64 * n:64 * n + 64] for n in range(2))
            y1, y2 = (rot[:, :, :].rearrange("p t (c e) -> p t c e", c=2)[:, :, :, 64 * n:64 * n + 64] for n in range(2))
            tm = kd[:, :, :].rearrange("p t (c e) -> p t c e", c=2)
            cs, sn = (const(n).rearrange("p (t a e) -> p t a e", a=1, e=64).to_broadcast([P, TT, 2, 64])
                      for n in ("cos", "sin"))
            with pool.Fori(0, RH) as r:
                own.enter(r, 6)
                pool.wait_ge(unit_free, r * B_UNITS + (3 + U_B + 5))
                pool.wait_ge(rt_free[1], r * 9 + 1)
                tt(y1, x1, cs, ALU.mult)
                own.after(tt(tm, x2, sn, ALU.mult))
                own.after(tt(y1, y1, tm, ALU.subtract))
                tt(y2, x1, sn, ALU.mult)
                own.after(tt(tm, x2, cs, ALU.mult))
                tt(y2, y2, tm, ALU.add).then_inc(rot_done, 1)
                pool.wait_ge(rot_done, r + 1)
                kdec = const("kdec")[:, bass.ds(r * TT, TT)].rearrange("p (t a) -> p t a", a=1).to_broadcast([P, TT, RK])
                tt(kd[:, :, :], rot[:, :, RK:2 * RK], kdec, ALU.mult).then_inc(kd_done, 1)
                pool.wait_ge(kd_done, r + 2)
                pool.wait_ge(rt_done, r * 18 + 3)
                tt(km.rearrange("p (b e) -> p b e", e=RK), kd[0:NS, QBLK:TT, :].to_broadcast([NS, DEC_B, RK]),
                   const("bmask", NS).rearrange("p (b a) -> p b a", a=1).to_broadcast([NS, DEC_B, RK]),
                   ALU.mult).then_inc(km_done, 1)
                pool.wait_ge(rt_free[1], r * 9 + 4)
                settle(pool)
                pool.dma_start(ret_p[0, bass.ds(r, 1), :, :].rearrange("r d e -> d (r e)"), schain[:, QBLK - 1, :])\
                    .then_inc(sc_stored, 16)
                for n in range(4):
                    pool.wait_ge(rt_free[n % 2], r * 9 + (7 + n // 2))
                    settle(pool)
                    dst = ret_s[2 * n:2 * n + 2, bass.ds(r, 1), :, :].rearrange("b r d e -> d (b r) e")
                    pool.dma_start(dst, st[:, 2 * n:2 * n + 2, :]).then_inc(st_stored, 16)
                pool.wait_ge(var_done, r + 1)
                settle(pool)
                own.after(pool.tensor_scalar(rstd[:, 0:QBLK], bmv[:, 0:QBLK, 1], EPS, None, ALU.add))
                own.after(tt(rstd[:, 0:QBLK], rstd[:, 0:QBLK], half[:, 0:QBLK], ALU.pow))
                settle(pool)
                own.after(pool.tensor_scalar(rstd[0:NS, QBLK:TT], bmv[0:NS, QBLK, 1:2], EPS, None, ALU.add))
                tt(rstd[0:NS, QBLK:TT], rstd[0:NS, QBLK:TT], half[0:NS, QBLK:TT], ALU.pow).then_inc(rstd_done, 1)
                pool.wait_ge(st_stored, r * 64 + 64)
                pool.wait_ge(sc_stored, r * 16 + 16)
                pool.sem_inc(states_out, 1)
                for s in range(2):
                    pool.wait_ge(w_high, r * (2 * B_CH) + (2 * C0_B + 4 + s + 1))
                    tt(wl[0][:, s * HW:(s + 1) * HW], wraw[s], wh[0][:, s * HW:(s + 1) * HW].bitcast(F32),
                       ALU.subtract).then_inc(w_low, 1)
            own.leave(RH)
            pool.sem_inc(b_end, 1)

            pool.wait_ge(br_free, 4 + 4 * KT_N)
            own.after(pool.memset(zhf[:, :], -0.5))
            for t in range(TT):
                m = P if t < QBLK else NS
                pool.wait_ge(zvar_done, t + 1)
                own.after(pool.tensor_scalar(zrs[0:m, t:t + 1], zmv[0:m, t, 1:2], EPS, None, ALU.add))
                tt(zrs[0:m, t:t + 1], zrs[0:m, t:t + 1], zhf[0:m, t:t + 1], ALU.pow).then_inc(zrstd_done, 1)

        @block.tensor
        def _(pe):
            def turn(out, in_):
                k = in_.shape[0]
                return pe.transpose(out, in_, ident[0:k, 0:k])

            def mm3(out, lhs, rhs, n):
                for k in range(n):
                    pe.matmul(out, lhs[0](k), rhs[0](k), start=(k == 0), stop=False)
                    pe.matmul(out, lhs[0](k), rhs[1](k), start=False, stop=False)
                    last = pe.matmul(out, lhs[1](k), rhs[0](k), start=False, stop=(k == n - 1))
                return last

            def tok(t):
                return slice(NS + t * P, NS + (t + 1) * P) if t < QBLK else slice(0, P)

            def chunk_ready(c):
                pe.wait_ge(w_low, c * 2 + 4)

            def weights(par, lo, n, width=CW):
                return [(lambda k, a=a: a[par][:, k * width + lo:k * width + lo + n]) for a in (wh, wl)]

            def halves(hi, lo, s):
                return [(lambda k, a=a: a[:, k, s * HALF:(s + 1) * HALF]) for a in (hi, lo)]

            def tiles(hi, lo, t):
                return [(lambda k, a=a: a[:, k, tok(t)]) for a in (hi, lo)]

            def natural(par, free, t, b):
                pe.wait_ge(unit_free, free)
                mm3(bank[b][:, 0:CW], tiles(xh, xl, t), weights(par, 0, CW), KT_N).then_inc(unit_done, 1)

            def transposed(par, free, n, s, b):
                pe.wait_ge(unit_free, free)
                mm3(bank[b][:, 0:HALF], weights(par, n * P, P), halves(xh, xl, s), KT_N).then_inc(unit_done, 1)

            pe.wait_ge(ident_in, 16)
            for k, b in X_ORDER:
                if k in (0, KT_N // 2):
                    pe.wait_ge(x_in[k // (KT_N // 2)], 16)
                if k is None:
                    pe.wait_ge(x_in[2], 16)
                    for n in range(KT_N):
                        last = turn(bank[b][:, n * NS:(n + 1) * NS], xn[0:NS, QBLK, n * P:(n + 1) * P])
                else:
                    if k == KT_N - 1:
                        pe.wait_ge(xh_done, 1)
                        pe.wait_ge(xl_done, 1)
                    for t in range(QBLK):
                        last = turn(bank[b][:, t * P:(t + 1) * P], xn[:, t, k * P:(k + 1) * P])
                last.then_inc(xt_done, 1)
            pe.wait_ge(xh_done, KT_N + 1)
            pe.wait_ge(xl_done, KT_N + 1)

            def attention_head(h):
                def unit(u):
                    return h * A_UNITS + (u + 3 if u == ZR_UNIT else u + 2)

                def group_free(n):
                    pe.wait_ge(tg_free[n % 2], h * (A_TG // 2) + (n // 2 + 1))
                    return bank[6 + n % 2]

                def group_read(n):
                    pe.wait_ge(tg_free[n % 2], h * (A_TG // 2) + (n // 2 + 2))

                def key_blocks(bi):
                    return [(0, k) for k in range(max(0, bi - 1), bi + 1)] + [(g, k) for g in (1, 2) for k in range(bi + 1)]

                def group_of(bi):
                    return (4, 5, 7, 9)[bi]

                def scores(bi):
                    pe.wait_ge(score_free, h * QBLK + (bi + 1))
                    for g in range(G):
                        lo = max(0, bi - 1) * P if g == 0 else 0
                        n = (bi + 1) * P - lo
                        last = pe.matmul(bank[3 + g][:, 0:n], qt[:, g, bi * P:(bi + 1) * P], kt[:, g, lo:lo + n],
                                         start=True, stop=True)
                    last.then_inc(score_done, 1)

                def probs_by_key(bi, lo=0, hi=12):
                    if lo == 0:
                        pe.wait_ge(exp_done, h * QBLK + (bi + 1))
                    nb = len(key_blocks(bi))
                    for x in range(lo, min(nb, hi)):
                        n = group_of(bi) + x // 4
                        if x % 4 == 0:
                            b = group_free(n)
                        last = turn(b[:, (x % 4) * P:(x % 4 + 1) * P], sp_[:, bi % 2, x * P:(x + 1) * P])
                        if x % 4 == 3 or x == nb - 1:
                            last.then_inc(tg_done, 1)

                def output(bi):
                    pe.wait_ge(o_read, h * QBLK + (bi + 1))
                    blocks = key_blocks(bi)
                    for x, (g, k) in enumerate(blocks):
                        if x % 4 == 0:
                            group_read(group_of(bi) + x // 4)
                        last = pe.matmul(bank[2][:, 0:P], pt[:, bi % 2, x * P:(x + 1) * P],
                                         kv[:, k, (G + g) * DH:(G + g + 1) * DH], start=(x == 0), stop=(x == len(blocks) - 1))
                    last.then_inc(o_done, 1)

                for j in range(2):
                    chunk_ready(h * A_CH + j)
                    for t in range(TT):
                        natural(j % 2, unit(5 * j + t), t, unit_bank(5 * j + t))

                def query_unit(u):
                    transposed(0, unit(u), (u - 10) // 2, u % 2, unit_bank(u))

                def q2_za_unit(u):
                    transposed(1, unit(u), (u - 14) // 2, u % 2, unit_bank(u))

                def value_unit(u):
                    natural(0, unit(u), u - 18, unit_bank(u))

                def zr_unit(u):
                    transposed(1, unit(u), (u - ZR_UNIT) // 2, (u - ZR_UNIT) % 2, unit_bank(u))

                chunk_ready(h * A_CH + 2)
                query_unit(10)
                pe.wait_ge(unit_free, h * A_UNITS + (3 + 10))
                for g in range(2):
                    b = group_free(g)
                    for t in range(QBLK):
                        last = turn(b[:, t * P:(t + 1) * P], kv[:, t, g * DH:(g + 1) * DH])
                    last.then_inc(tg_done, 1)
                for u in (11, 12, 13):
                    query_unit(u)
                b = group_free(2)
                for t in range(QBLK):
                    last = turn(b[:, t * P:(t + 1) * P], kv[:, t, 2 * DH:3 * DH])
                last.then_inc(tg_done, 1)
                b = group_free(3)
                settle(pe)
                for g in range(G):
                    last = turn(b[:, g * NS:(g + 1) * NS], ks[:, g * DH:(g + 1) * DH])
                last.then_inc(tg_done, 1)
                chunk_ready(h * A_CH + 3)
                for u in (14, 15, 16):
                    q2_za_unit(u)
                group_read(2)
                group_read(3)
                pe.wait_ge(unit_free, h * A_UNITS + (3 + 16))
                scores(0)
                q2_za_unit(17)
                scores(1)
                chunk_ready(h * A_CH + 4)
                value_unit(18)
                value_unit(19)
                probs_by_key(0)
                value_unit(20)
                scores(2)
                value_unit(21)
                probs_by_key(1)
                value_unit(22)
                scores(3)
                chunk_ready(h * A_CH + 5)
                zr_unit(23)
                pe.wait_ge(unit_free, h * A_UNITS + (3 + 23))
                output(0)
                probs_by_key(2)
                output(1)
                zr_unit(24)
                probs_by_key(3, 0, 8)
                output(2)
                probs_by_key(3, 8)
                zr_unit(25)
                output(3)
                zr_unit(26)
                for n in range(2):
                    pe.wait_ge(o_read, h * QBLK + (2 * n + 3))
                    b = group_free(12 + n)
                    for x in range(2):
                        last = turn(b[:, x * P:(x + 1) * P], on[:, 2 * n + x, :])
                    last.then_inc(tg_done, 1)

            with pe.Fori(0, H) as h:
                attention_head(h)
            pe.wait_ge(unit_free, 3 + U_B)
            for b in range(2):
                pe.wait_ge(tg_free[b], TB_B + 1)
            pe.matmul(bank[7][:, 0:1], ident, ident[:, 0:1], start=True, stop=True).then_inc(a_end, 1)
            pe.wait_ge(a_end, 4)

            def retention_head(r):
                def unit(u):
                    return r * B_UNITS + (U_B + u + 2)

                def transpose_tile(x, j):
                    for n, (lo, hi) in enumerate(SLOTS):
                        if j == lo:
                            pe.wait_ge(slot_in[n], r * 128 + (64 * x + 32))
                            settle(pe)
                        if lo <= j < hi:
                            s, k = n, j - lo
                    if j >= 2:
                        pe.wait_ge(part_low, r * 52 + (26 * x + 26 + j - 1))
                    for h in range(H):
                        last = turn(bank[2 + j % 2][:, h * P:(h + 1) * P], cslot[s][:, k, h * DH:(h + 1) * DH])
                    last.then_inc(tg_done, 1)

                def cached_scores(x):
                    def score_tile(j):
                        pe.wait_ge(part_low, r * 52 + (26 * x + 26 + j + 1))
                        if j == 9:
                            pe.wait_ge(qm_done, r * 4 + (2 * x + 2))
                            settle(pe)
                        g, m, block = (0, 0, 0) if j == 0 else (1, j - 1, 12) if j < 5 else (2, j - 5, 28 if j < 9 else 12 - 16)
                        for h in range(H):
                            o = (block + m * H + h) * BLK
                            for i, part in enumerate((part_h, part_l)):
                                last = pe.matmul(bank[4][0:BLK, g * P:(g + 1) * P], qm[:, o:o + BLK],
                                                 part[j % 3][:, h * P:(h + 1) * P], start=(m == 0 and h == 0 and i == 0),
                                                 stop=(j in (0, 4, 12) and h == H - 1 and i == 1))
                        last.then_inc(part_used, 1)

                    pe.wait_ge(co_read, r * 2 + (x + 1))
                    settle(pe)
                    pe.wait_ge(qm_done, r * 4 + (2 * x + 1))
                    settle(pe)
                    for j in range(TILES):
                        if j + 2 < TILES:
                            transpose_tile(x, j + 2)
                        score_tile(j)
                    for g in range(G):
                        for h in range(H):
                            o = (g * H + h) * BLK
                            last = pe.matmul(bank[5][0:BLK, g * NS:(g + 1) * NS], qm[:, o:o + BLK].bitcast(F32),
                                             ktn[:, (h * G + g) * NS:(h * G + g + 1) * NS], start=(h == 0), stop=(h == H - 1))
                    last.then_inc(cs_done, 1)

                def cached_probs(x):
                    pe.wait_ge(rows_norm, r * 2 + (x + 1))
                    settle(pe)
                    for g in range(G):
                        turn(bank[5][:, 192 + g * ROWS:192 + (g + 1) * ROWS], srow[:, g * P:(g + 1) * P])
                        last = turn(bank[5][0:NS, 288 + g * ROWS:288 + (g + 1) * ROWS],
                                    srow[:, 384 + g * NS:384 + (g + 1) * NS])
                    last.then_inc(cp_done, 1)

                def cached_output(x):
                    pe.wait_ge(cp_read, r * 2 + (x + 1))
                    settle(pe)
                    for i in range(TILES):
                        pe.wait_ge(part_low, r * 52 + (26 * x + 26 + TILES + i + 1))
                        for part in (part_h, part_l):
                            last = pe.matmul(bank[4][0:BLK, :], pm[:, i * BLK:(i + 1) * BLK], part[i % 3][:, :],
                                             start=(i == 0 and part is part_h), stop=False)
                        last.then_inc(part_used, 1)
                    new = vn[:, :].rearrange("p (h g e) -> p h g e", g=G, e=DH)
                    for g in range(G):
                        last = pe.matmul(bank[4][0:BLK, :], pn[:, g * BLK:(g + 1) * BLK], new[:, :, g, :],
                                         start=False, stop=(g == G - 1))
                    last.then_inc(co_done, 1)

                def cached_turn(x):
                    pe.wait_ge(co_sum, r * 2 + (x + 1))
                    settle(pe)
                    for h in range(H):
                        last = turn(bank[5][:, 384 + h * ROWS:384 + (h + 1) * ROWS], srow[:, h * DH:(h + 1) * DH])
                    last.then_inc(ct_done, 1)

                def group(n):
                    pe.wait_ge(rt_free[n % 2], r * 9 + (n // 2 + 1))
                    return bank[6 + n % 2]

                def group_read(n):
                    pe.wait_ge(rt_free[n % 2], r * 9 + (n // 2 + 2))

                def blocks(f, n=QBLK):
                    for t in range(n):
                        last = f(t, slice(t * P, (t + 1) * P))
                    last.then_inc(rt_done, 1)

                def att_group():
                    group_read(0)
                    group_read(1)
                    b = group(3)
                    blocks(lambda t, c: pe.matmul(b[:, c], krt[:, c], qrt[:, c], start=True, stop=True))

                def state_group(n):
                    b = group(4 + n)
                    for t in range(2):
                        last = pe.matmul(b[:, t * RV:(t + 1) * RV], kd[:, 2 * n + t, :], vr[:, 2 * n + t, :],
                                         start=True, stop=True)
                    last.then_inc(rt_done, 1)

                def sample_state_group(n):
                    b = group(10 + n)
                    for x in range(2):
                        o = (2 * n + x) * RK
                        last = pe.matmul(b[:, x * RV:(x + 1) * RV], km[:, o:o + RK], vr[0:NS, QBLK, :],
                                         start=True, stop=True)
                    last.then_inc(rt_done, 1)

                transpose_tile(0, 0)
                transpose_tile(0, 1)
                chunk_ready(r * B_CH + C0_B)
                natural(0, unit(0), 0, 0)
                cached_scores(0)
                for t in range(1, TT):
                    if t == 3:
                        cached_probs(0)
                    natural(0, unit(t), t, t % 2)
                chunk_ready(r * B_CH + (C0_B + 1))
                for t in range(TT):
                    natural(1, unit(5 + t), t, (5 + t) % 2)
                pe.wait_ge(rot_done, r + 1)
                b = group(0)
                blocks(lambda t, c: turn(b[:, c], rot[:, t, 0:RK]))
                b = group(1)
                blocks(lambda t, c: turn(b[:, c], rot[:, t, RK:2 * RK]))
                cached_output(0)
                b = group(2)
                settle(pe)
                turn(b[:, 0:NS], rot[0:NS, QBLK, 0:RK])
                turn(b[:, NS:2 * NS], rot[0:NS, QBLK, RK:2 * RK]).then_inc(rt_done, 1)
                att_group()
                pe.wait_ge(kd_done, r + 2)
                pe.wait_ge(unit_free, r * B_UNITS + (3 + U_B + 10))
                state_group(0)
                transpose_tile(1, 0)
                state_group(1)
                transpose_tile(1, 1)
                cached_turn(0)
                group_read(2)
                b = group(6)
                pe.matmul(b[0:NS, 0:NS], qkts[:, NS:2 * NS], qkts[:, 0:NS], start=True, stop=True).then_inc(rt_done, 1)
                cached_scores(1)
                group_read(3)
                group_read(4)
                for n in range(2):
                    b = group(7 + n)
                    if n == 0:
                        group_read(5)
                    for t in range(2 * n, 2 * n + 2):
                        o = b[:, (t % 2) * RV:(t % 2 + 1) * RV]
                        last = pe.matmul(o, krt[:, t * P:(t + 1) * P], vr[:, t, :], start=True, stop=(t == 0))
                        if t:
                            last = pe.matmul(o, qdt[:, t * P:(t + 1) * P], schain[:, t - 1, :], start=False, stop=True)
                    last.then_inc(rt_done, 1)
                group_read(6)
                pe.wait_ge(st_in, r * 16 + 16)
                b = group(9)
                settle(pe)
                pe.matmul(b[0:NS, 0:RV], atts[:, :], vr[0:NS, QBLK, :], start=True, stop=False)
                for n in range(DEC_B):
                    last = pe.matmul(b[0:NS, 0:RV], qdm[:, n * NS:(n + 1) * NS], st[:, n, :],
                                     start=False, stop=(n == DEC_B - 1))
                last.then_inc(rt_done, 1)
                pe.wait_ge(km_done, r + 1)
                sample_state_group(0)
                sample_state_group(1)
                cached_probs(1)
                sample_state_group(2)
                sample_state_group(3)
                cached_output(1)
                pe.wait_ge(normed, r + 1)
                for e in range(2):
                    b = group(14 + e)
                    blocks(lambda t, c: turn(b[:, c], qk[:, t, e * P:(e + 1) * P]))
                for e in range(2):
                    b = group(16 + e)
                    settle(pe)
                    turn(b[:, 0:NS], qk[0:NS, QBLK, e * P:(e + 1) * P]).then_inc(rt_done, 1)
                cached_turn(1)

            with pe.Fori(0, RH) as r:
                retention_head(r)
            for b in range(2):
                pe.wait_ge(rt_free[b], RH * 9 + 1)
            pe.wait_ge(co_read, 2 * RH + 1)
            pe.matmul(bank[0][:, 0:1], ident, ident[:, 0:1], start=True, stop=True).then_inc(b_end, 1)
            pe.wait_ge(b_end, 4)

            def feature_tile(f):
                chunk_ready(f * C_CH + C0_C)
                for u in range(4):
                    pe.wait_ge(gt_free, f * 4 + (u + 1))
                    mm3(bank[u][:, 0:HALF], weights(0, (u // 2) * P, P), halves(xh, xl, u % 2), KT_N).then_inc(gt_done, 1)
                chunk_ready(f * C_CH + (C0_C + 1))
                pe.wait_ge(split_h, 2)
                pe.wait_ge(split_l, 2)
                for u in range(4):
                    pe.wait_ge(br_free, f * 4 + (u + 1))
                    hi, lo, k0, n = (oah, oal, 0, H) if u < 2 else (ybh, ybl, H, 2 * RH)
                    w = [(lambda k, a=a: a[1][:, (k + k0) // 6 * HW + (k + k0) % 6 * P:][:, 0:P]) for a in (wh, wl)]
                    mm3(bank[4 + u][:, 0:HALF], w, halves(hi, lo, u % 2), n).then_inc(br_done, 1)

            with pe.Fori(0, KT_N) as f:
                feature_tile(f)
            pe.wait_ge(gt_free, 4 + 4 * KT_N)
            pe.wait_ge(br_free, 4 + 4 * KT_N)
            pe.wait_ge(ul_done, KT_N)
            for n in range(4):
                chunk_ready(C0_O + n)
                for t in range(TT):
                    v = n * TT + t
                    if v >= 8:
                        pe.wait_ge(ou_free, v - 7)
                    mm3(bank[v % 8][:, 0:CW], tiles(uh, ul, t), weights(n % 2, 0, CW), KT_N).then_inc(ou_done, 1)

        @block.scalar
        def _(act):
            def high(c, par, used, n=HW, halves=(0, 1)):
                for s in halves:
                    act.wait_ge(w_in_s[s], c * 32 + 32)
                    if s == 0:
                        used()
                    act.activation(wh[par][:, s * HW:s * HW + n], wraw[s][:, 0:n], ACT.Copy).then_inc(w_high, 1)

            act.wait_ge(credits, 1)
            for n, (k, b) in enumerate(X_ORDER):
                act.wait_ge(xt_done, n + 1)
                if k is None:
                    act.activation(xh[:, :, 0:NS], bank[b][:, :].rearrange("p (k n) -> p k n", n=NS), ACT.Copy)\
                        .then_inc(xh_done, 1)
                else:
                    act.activation(xh[:, k, NS:NTOK], bank[b][:, :], ACT.Copy).then_inc(xh_done, 1)
                if k == KT_N // 2 - 1:
                    high(0, 0, lambda: None, halves=(0,))
            high(0, 0, lambda: None, halves=(1,))

            def attention_head(h):
                def group(n, out, width):
                    act.wait_ge(tg_done, h * A_TG + (TD + n + 1))
                    act.activation(out, bank[6 + n % 2][:, 0:width], ACT.Copy).then_inc(tg_free[n % 2], 1)

                def sigmoid(u, n):
                    act.wait_ge(unit_done, h * A_UNITS + (UD + u + 1))
                    act.wait_ge(gate_free, h * 6 + (n + 1))
                    act.activation(sg[:, n % 2, :], bank[unit_bank(u)][:, 0:HALF], ACT.Sigmoid).then_inc(gate_sig, 1)

                def exponential(bi):
                    act.wait_ge(max_done, h * QBLK + (bi + 1))
                    n = min(2, bi + 1) * P + 2 * (bi + 1) * P
                    act.activation(sp_[:, bi % 2, 0:n], sp_[:, bi % 2, 0:n], ACT.Exp, bias=nmax[:, bi:bi + 1],
                                   accum_out=rsum[:, bi:bi + 1]).then_inc(exp_done, 1)

                def probs(bi, n):
                    nb = min(2, bi + 1) + 2 * (bi + 1)
                    x = (n - (4, 5, 7, 9)[bi]) * 4
                    w = min(4, nb - x) * P
                    group(n, pt[:, bi % 2, x * P:x * P + w], w)

                def next_high(j):
                    at = (-4, 0, 5, 10, 14, 18)[(j + 1) % 6]
                    more = 27 if j == 5 else 0
                    high(h * A_CH + (j + 1), (j + 1) % 2,
                         lambda: act.wait_ge(unit_done, h * A_UNITS + (UD + at + more)))

                next_high(0)
                next_high(1)
                group(0, kt[:, 0, :], SEQ)
                next_high(2)
                group(2, kt[:, 2, :], SEQ)
                next_high(3)
                sigmoid(16, 0)
                sigmoid(17, 1)
                exponential(0)
                exponential(1)
                next_high(4)
                probs(0, 4)
                exponential(2)
                probs(1, 6)
                next_high(5)
                sigmoid(23, 2)
                probs(2, 8)
                exponential(3)
                sigmoid(24, 3)
                probs(3, 10)
                sigmoid(25, 4)
                sigmoid(26, 5)

            with act.Fori(0, H) as h:
                attention_head(h)
            act.sem_inc(a_end, 1)

            def retention_head(r):
                def used_b(n):
                    return lambda: act.wait_ge(unit_done, r * B_UNITS + (UD + U_B + n))

                def keys(x):
                    for j in range(TILES):
                        act.wait_ge(part_used, r * 52 + (26 * x + (1 if j < 3 else j - 1)))
                        settle(act)
                        act.wait_ge(tg_done, r * B_TG + (TG_B + 13 * x + j + 1))
                        act.activation(part_h[j % 3][:, :], bank[2 + j % 2][:, :], ACT.Copy).then_inc(part_high, 1)

                def values(x, first, end):
                    for i in range(first, end):
                        act.wait_ge(part_used, r * 52 + (26 * x + TILES + (1 if i < 3 else i - 1)))
                        settle(act)
                        for n, (lo, hi) in enumerate(SLOTS):
                            if i == lo:
                                act.wait_ge(slot_in[n], r * 128 + (64 * x + 64))
                                settle(act)
                            if lo <= i < hi:
                                s, k = n, i - lo
                        act.activation(part_h[i % 3][:, :], cslot[s][:, k, :], ACT.Copy).then_inc(part_high, 1)

                def rows(x):
                    act.wait_ge(rows_max, r * 2 + (x + 1))
                    act.activation(srow[:, :], srow[:, :], ACT.Exp, bias=smx[:, 0:1], accum_out=smx[:, 1:2])\
                        .then_inc(rows_exp, 1)

                def output_lows(x):
                    act.wait_ge(co_done, r * 2 + (x + 1))
                    act.activation(srow[:, 0:512], bank[4][ROWS:BLK, :], ACT.Copy).then_inc(co_lows, 1)

                def group(n, out, in_):
                    act.wait_ge(rt_done, r * 18 + (n + 1))
                    act.activation(out, in_, ACT.Copy).then_inc(rt_free[n % 2], 1)

                keys(0)
                rows(0)
                values(0, 0, 3)
                high(r * B_CH + (C0_B + 1), 1, used_b(0))
                group(1, krt[:, :], bank[7][:, :])
                values(0, 3, TILES)
                output_lows(0)
                keys(1)
                values(1, 0, 3)
                rows(1)
                group(7, qk[:, 0:2, :], bank[7][:, :].rearrange("p (t e) -> p t e", e=RV))
                group(8, qk[:, 2:4, :], bank[6][:, :].rearrange("p (t e) -> p t e", e=RV))
                values(1, 3, TILES)
                output_lows(1)
                high(r * B_CH + (C0_B + 2), 0, used_b(5))

            act.wait_ge(a_end, 4)
            with act.Fori(0, RH) as r:
                retention_head(r)
            act.sem_inc(b_end, 1)
            act.wait_ge(b_end, 4)

            act.activation(oah[:, :, :].rearrange("p k n -> p (k n)"), oa[:, :], ACT.Copy).then_inc(split_h, 1)
            act.activation(ybh[:, :, :].rearrange("p k n -> p (k n)"), yb[:, :], ACT.Copy).then_inc(split_h, 1)
            act.wait_ge(split_l, 2)
            with act.Fori(0, KT_N) as f:
                high(f * C_CH + (C0_C + 1), 1, lambda: act.wait_ge(br_done, f * 4 + 1), 6 * P)
                act.wait_ge(u_done, f + 1)
                for u in range(4):
                    act.wait_ge(gt_done, f * 4 + (u + 1))
                    act.activation(sgc[:, u // 2, (u % 2) * HALF:(u % 2 + 1) * HALF], bank[u][:, 0:HALF], ACT.Sigmoid)\
                        .then_inc(gt_free, 1)
                high(f * C_CH + (C0_C + 2), 0, lambda: act.wait_ge(gt_done, f * 4 + 4))
                act.wait_ge(u_done, f + 2)
                act.activation(uh[:, bass.ds(f, 1), :].rearrange("p k n -> p (k n)"), uc[:, 0, :], ACT.Copy)\
                    .then_inc(uh_done, 1)
            high(C0_O + 1, 1, lambda: act.wait_ge(br_done, 1 + 4 * KT_N))
            high(C0_O + 2, 0, lambda: act.wait_ge(ou_done, TT))
            high(C0_O + 3, 1, lambda: act.wait_ge(ou_done, 2 * TT))
            for t in range(TT):
                m = P if t < QBLK else NS
                act.wait_ge(y_done, t + 1)
                dst = y_prompt[0, t * P:(t + 1) * P, :] if t < QBLK else y_sample.rearrange("b t d -> (b t) d")
                act.dma_start(dst, z[0:m, t, :]).then_inc(y_stored, 16)
            act.wait_ge(y_stored, 16 * TT)

        @block.vector
        def _(dve):
            own = Links(dve, dve_l)
            tt = dve.tensor_tensor

            def low(c, par, n=HW, halves=(0, 1)):
                for s in halves:
                    dve.wait_ge(w_high, c * 2 + (s + 1))
                    tt(wl[par][:, s * HW:s * HW + n], wraw[s][:, 0:n], wh[par][:, s * HW:s * HW + n].bitcast(F32),
                       ALU.subtract).then_inc(w_low, 1)

            dve.wait_ge(credits, 1)
            for n, (k, b) in enumerate(X_ORDER):
                dve.wait_ge(xh_done, n + 1)
                if k is None:
                    tt(xl[:, :, 0:NS], bank[b][:, :].rearrange("p (k n) -> p k n", n=NS), xh[:, :, 0:NS].bitcast(F32),
                       ALU.subtract).then_inc(xl_done, 1)
                else:
                    tt(xl[:, k, NS:NTOK], bank[b][:, :], xh[:, k, NS:NTOK].bitcast(F32), ALU.subtract).then_inc(xl_done, 1)
                if k == KT_N // 2 - 1:
                    low(0, 0, halves=(0,))
            low(0, 0, halves=(1,))
            dve.wait_ge(con_in, 16)
            dve.wait_ge(nd_in, 16)

            def attention_head(h):
                def unit(u):
                    dve.wait_ge(unit_done, h * A_UNITS + (UD + u + 1))
                    return bank[unit_bank(u)]

                def group(n):
                    dve.wait_ge(tg_done, h * A_TG + (TD + n + 1))
                    return bank[6 + n % 2]

                def queries(u, g, s):
                    b = unit(u)
                    if s == 0:
                        dve.tensor_scalar(qts[:, bass.ds(h * (G * NS) + g * NS, NS)], b[:, 0:NS], SCALE, None, ALU.mult)
                        dve.tensor_scalar(qt[:, g, 0:HALF - NS], b[:, NS:HALF], SCALE, None, ALU.mult).then_inc(unit_free, 1)
                    else:
                        dve.tensor_scalar(qt[:, g, HALF - NS:SEQ], b[:, 0:HALF], SCALE, None, ALU.mult).then_inc(unit_free, 1)

                def silu(u, n, out):
                    b = unit(u)
                    dve.wait_ge(gate_sig, h * 6 + (n + 1))
                    tt(out, b[:, 0:HALF], sg[:, n % 2, :], ALU.mult).then_inc(unit_free, 1)
                    dve.wait_ge(unit_free, h * A_UNITS + (3 + u + 1))
                    dve.sem_inc(gate_free, 1)

                def keys_values(u, t, lo):
                    b = unit(u)
                    if t < QBLK:
                        dve.tensor_copy(kv[:, t, lo:lo + CW], b[:, 0:CW]).then_inc(unit_free, 1)
                        return
                    nk = max(0, min(CW, G * DH - lo))
                    if nk:
                        i = dve.tensor_copy(ks[:, lo:lo + nk], b[0:NS, 0:nk])
                    if nk < CW:
                        i = dve.tensor_copy(vn[:, bass.ds(h * (G * DH) + (lo + nk - G * DH), CW - nk)], b[0:NS, nk:CW])
                    i.then_inc(unit_free, 1)

                def softmax(bi):
                    dve.wait_ge(score_done, h * QBLK + (bi + 1))
                    dve.wait_ge(tg_done, h * A_TG + (TD + (-5, -2, 5, 7)[bi]))
                    o = 0
                    for g in range(G):
                        n = (min(2, bi + 1) if g == 0 else bi + 1) * P
                        end = ND_O[g] + ND_W[g]
                        i = dve.scalar_tensor_tensor(
                            out=sp_[:, bi % 2, o:o + n], in0=nd[:, end - n:end],
                            scalar=const("slopes")[:, bass.ds(h * G + g, 1)], in1=bank[3 + g][:, 0:n],
                            op0=ALU.mult, op1=ALU.add)
                        o += n
                    i.then_inc(score_free, 1)
                    dve.wait_ge(score_free, h * QBLK + (bi + 2))
                    dve.tensor_reduce(nmax[:, bi:bi + 1], sp_[:, bi % 2, 0:o], AX.X, ALU.max, negate=True)\
                        .then_inc(max_done, 1)

                def probs(bi, n):
                    nb = min(2, bi + 1) + 2 * (bi + 1)
                    x = (n - (4, 5, 7, 9)[bi]) * 4
                    w = min(4, nb - x) * P
                    b = group(n)
                    dve.tensor_copy(pt[:, bi % 2, x * P:x * P + w], b[:, 0:w]).then_inc(tg_free[n % 2], 1)

                def output(bi):
                    dve.wait_ge(exp_done, h * QBLK + (bi + 1))
                    own.after(dve.reciprocal(rinv[:, bi:bi + 1], rsum[:, bi:bi + 1]))
                    dve.wait_ge(o_done, h * QBLK + (bi + 1))
                    dve.tensor_scalar(on[:, bi, :], bank[2][:, 0:P], rinv[:, bi:bi + 1], None, ALU.mult)\
                        .then_inc(o_read, 1)

                c = h * A_CH
                dve.wait_ge(kv_out, h + 1)
                for j in range(2):
                    low(c + (j + 1), (j + 1) % 2)
                    for t in range(TT):
                        keys_values(5 * j + t, t, CW * j)
                queries(10, 0, 0)
                b = group(1)
                dve.tensor_copy(kt[:, 1, :], b[:, :]).then_inc(tg_free[1], 1)
                low(c + 3, 1)
                for u in range(1, 4):
                    queries(10 + u, u // 2, u % 2)
                b = group(3)
                dve.tensor_copy(ktn[:, bass.ds(h * (G * NS), G * NS)], b[:, 0:G * NS]).then_inc(tg_free[1], 1)
                low(c + 4, 0)
                queries(14, 2, 0)
                queries(15, 2, 1)

                def za(n):
                    silu(16 + n, n, oa[:, bass.ds(h * NTOK + n * HALF, HALF)])

                def zr(n):
                    silu(23 + n, 2 + n, yb[:, bass.ds(h * (2 * NTOK) + n * HALF, HALF)])

                def values(u):
                    keys_values(u, u - 18, 2 * CW)

                za(0)
                softmax(0)
                za(1)
                softmax(1)
                values(18)
                values(19)
                low(c + 5, 1)
                values(20)
                softmax(2)
                values(21)
                probs(1, 5)
                values(22)
                softmax(3)
                zr(0)
                output(0)
                probs(2, 7)
                output(1)
                low(c + 6, 0)
                zr(1)
                probs(3, 9)
                output(2)
                probs(3, 11)
                zr(2)
                output(3)
                zr(3)
                for n in range(2):
                    b = group(12 + n)
                    o = oa[:, bass.ds(h * NTOK + (NS + 2 * n * P), 2 * P)]
                    tt(o, b[:, 0:2 * P], o, ALU.mult).then_inc(tg_free[n % 2], 1)

            with dve.Fori(0, H) as h:
                own.enter(h, 4)
                attention_head(h)
            own.leave(H)
            dve.wait_ge(tg_free[1], TB_B + 1)
            dve.sem_inc(a_end, 1)
            dve.wait_ge(a_end, 4)
            dve.wait_ge(gn_in, 16)
            dve.wait_ge(kd_done, 1)
            for a in (qm, pm):
                n = a.shape[1]
                for o in range(0, n, DEC_B * NS):
                    w = min(n - o, DEC_B * NS)
                    i = dve.tensor_copy(a[:, o:o + w], qdm[:, 0:w])
            own.after(i)

            oav = oa[:, :].rearrange("p (h n) -> p h n", n=NTOK)

            def retention_head(r):
                def unit(u):
                    dve.wait_ge(unit_done, r * B_UNITS + (UD + U_B + u + 1))
                    return bank[u % 2]

                def group(n):
                    dve.wait_ge(rt_done, r * 18 + (n + 1))
                    return bank[6 + n % 2]

                def lows(x, which, first, end, between=()):
                    for i in range(first, end):
                        for tile, work in between:
                            if i == tile:
                                work()
                        dve.wait_ge(part_high, r * 52 + (26 * x + TILES * which + i + 1))
                        if which == 0:
                            src = bank[2 + i % 2]
                        else:
                            for n, (lo, hi) in enumerate(SLOTS):
                                if lo <= i < hi:
                                    src = cslot[n][:, i - lo, :]
                        tt(part_l[i % 3][:, :], src[:, :], part_h[i % 3][:, :].bitcast(F32), ALU.subtract)\
                            .then_inc(part_low, 1)

                def at(a, o, *dims):
                    a = a[:, o:o + 1]
                    return bass.AP(tensor=a.tensor, offset=a.offset, ap=[a.ap[0], *[list(d) for d in dims]])

                def place(pieces, of):
                    for o, dims, src in pieces:
                        i = dve.tensor_copy(at(of, o, *dims), src)
                    own.after(i)
                    for o, dims, src in pieces:
                        i = tt(at(of, o + ROWS, *dims), src, at(of, o, *dims).bitcast(F32), ALU.subtract)
                    return i

                def of(x, g):
                    src = qts[:, :].rearrange("p (h g b q) -> p g h b q", g=G, b=DEC_B, q=DEC_T)
                    return src[:, g, :, bass.ds(r * 2 + x, 1), :].rearrange("p h b q -> p h (b q)")

                def residues(block, e, src):
                    return (block * BLK + 4 * e, ((H * BLK + 1, 4), (BLK + DEC_T, H)),
                            src[:, :, 4 * e:4 * e + 4].rearrange("p h j -> p j h"))

                def queries(x):
                    dve.wait_ge(cs_done, r * 2 + (x + 1))
                    settle(dve)
                    place([(g * H * BLK, ((BLK + DEC_T, H), (1, DEC_T)), of(x, g)) for g in range(G)]
                          + [residues(12, e, of(x, 1)) for e in range(2)] + [residues(28, 0, of(x, 2))], qm)\
                        .then_inc(qm_done, 1)

                def queries_4_to_7(x):
                    dve.wait_ge(part_used, r * 52 + (26 * x + 1 + 5))
                    settle(dve)
                    for part in range(2):
                        o, dims, _ = residues(12, 0, of(x, 1))
                        a = at(qm, o + part * ROWS, *dims)
                        tt(a, a.bitcast(F32), a.bitcast(F32), ALU.subtract)
                    place([residues(12, 1, of(x, 2))], qm).then_inc(qm_done, 1)

                def rows(x):
                    dve.wait_ge(cs_done, r * 2 + (x + 2))
                    settle(dve)
                    cached, new = srow[:, 0:384], srow[:, 384:576].rearrange("p (g n) -> p g n", g=G)
                    bn = const("biasn", ROWS).rearrange("p (g n) -> p g n", g=G)[:, :, bass.ds(r * -16 + (56 - 8 * x), NS)]
                    tt(cached, bank[4][0:ROWS, 0:384], const("biasc", ROWS), ALU.add)
                    own.after(tt(new, bank[5][0:ROWS, 0:G * NS].rearrange("p (g n) -> p g n", g=G), bn, ALU.add))
                    tt(cached, bank[4][ROWS:BLK, 0:384], cached, ALU.add)
                    own.after(tt(srow[:, 384:576], bank[5][ROWS:BLK, 0:G * NS], srow[:, 384:576], ALU.add))
                    dve.tensor_reduce(smx[:, 0:1], srow[:, :], AX.X, ALU.max, negate=True).then_inc(rows_max, 1)

                def probs(x):
                    dve.wait_ge(cp_done, r * 2 + (x + 1))
                    settle(dve)
                    place([(0, ((1, ROWS),), bank[5][:, 192:192 + ROWS]),
                           (BLK, ((BLK + 1, 4), (4, 2 * H)), at(bank[5], 224, (1, 4), (4, 2 * H))),
                           (5 * BLK, ((BLK + 1, DEC_T), (DEC_T, H)), at(bank[5], 256, (1, DEC_T), (DEC_T, H)))], pm)
                    dve.tensor_copy(pn[:, :].rearrange("p (g n) -> p g n", g=G)[:, :, 0:ROWS],
                                    bank[5][0:NS, 288:384].rearrange("p (g n) -> p g n", g=G)).then_inc(cp_read, 1)

                def normalise_rows(x):
                    dve.wait_ge(rows_exp, r * 2 + (x + 1))
                    own.after(dve.reciprocal(smx[:, 2:3], smx[:, 1:2]))
                    dve.tensor_scalar(srow[:, :], srow[:, :], smx[:, 2:3], None, ALU.mult).then_inc(rows_norm, 1)

                def output_sum(x):
                    dve.wait_ge(co_lows, r * 2 + (x + 1))
                    tt(srow[:, 0:512], bank[4][0:ROWS, :], srow[:, 0:512], ALU.add).then_inc(co_sum, 1)

                def output(x):
                    dve.wait_ge(ct_done, r * 2 + (x + 1))
                    o = oav[:, :, bass.ds(r * 16 + 8 * x, DEC_T)]
                    b = bank[5][:, 384:385]
                    b = bass.AP(tensor=b.tensor, offset=b.offset, ap=[b.ap[0], [ROWS + DEC_T, H], [1, DEC_T]])
                    tt(o, b, o, ALU.mult).then_inc(co_read, 1)

                def values(t):
                    b = unit(5 + t)
                    m = P if t < QBLK else NS
                    dve.tensor_copy(vr[0:m, t, :], b[0:m, 0:RV]).then_inc(unit_free, 1)

                def projected(t):
                    b = unit(t)
                    m = P if t < QBLK else NS
                    dve.tensor_copy(qk[0:m, t, :], b[0:m, 0:2 * RK]).then_inc(unit_free, 1)

                def sample_states(n):
                    b = group(10 + n)
                    s = st[:, 2 * n:2 * n + 2, :]
                    dve.scalar_tensor_tensor(out=s, in0=s, scalar=const("cdec")[:, bass.ds(r * 2 + 1, 1)],
                                             in1=b[:, :].rearrange("p (b e) -> p b e", e=RV), op0=ALU.mult,
                                             op1=ALU.add).then_inc(rt_free[n % 2], 1)

                def prompt_statistics():
                    dve.wait_ge(rt_free[1], r * 9 + 5)
                    dve.wait_ge(rt_free[0], r * 9 + 6)
                    settle(dve)
                    for t in range(QBLK):
                        dve.bn_stats(bst[:, t, :], qk[:, t, :])

                def sample_statistics():
                    dve.wait_ge(rt_free[1], r * 9 + 6)
                    own.after(dve.bn_stats(bst[0:NS, QBLK, :], qk[0:NS, QBLK, :]))
                    settle(dve)
                    for t in range(TT):
                        m = P if t < QBLK else NS
                        i = dve.bn_aggr(bmv[0:m, t, :], bst[0:m, t, :])
                    i.then_inc(var_done, 1)

                def normalise():
                    dve.wait_ge(rstd_done, r + 1)
                    for t in range(TT):
                        m = P if t < QBLK else NS
                        i = dve.tensor_scalar(qk[0:m, t, :], qk[0:m, t, :], bmv[0:m, t, 0:1], rstd[0:m, t:t + 1],
                                              ALU.subtract, ALU.mult)
                    i.then_inc(normed, 1)

                lows(0, 0, 0, 2)
                queries(0)
                projected(0)
                lows(0, 0, 2, TILES, [(7, lambda: queries_4_to_7(0))])
                rows(0)
                projected(1)
                normalise_rows(0)
                projected(2)
                probs(0)
                projected(3)
                dve.wait_ge(w_low, r * (2 * B_CH) + (2 * C0_B + 4))
                settle(dve)
                low(r * B_CH + (C0_B + 1), 1)
                projected(4)
                values(0)
                queries(1)
                values(1)
                lows(0, 1, 0, 3)
                for t in (2, 3, 4):
                    values(t)
                b = group(0)
                dve.tensor_copy(qrt[:, :], b[:, :])
                qdec = const("qdec").rearrange("p (r a n) -> p r a n", a=1, n=P)[:, bass.ds(r, 1), :, :]
                tt(qdt[:, :].rearrange("p (t n) -> p t n", n=P), b[:, :].rearrange("p (t n) -> p t n", n=P),
                   qdec.rearrange("p r a n -> p (r a) n").to_broadcast([P, QBLK, P]), ALU.mult).then_inc(rt_free[0], 1)
                lows(0, 1, 3, TILES)
                b = group(2)
                dve.tensor_copy(qkts, b[:, 0:2 * NS])
                diag = qdm[:, 0:DEC_B * NS]
                diag = bass.AP(tensor=diag.tensor, offset=diag.offset, ap=[diag.ap[0], [NS + DEC_T, DEC_B], [1, DEC_T]])
                tt(diag, b[:, 0:NS].rearrange("p (b q) -> p b q", q=DEC_T),
                   const("qdec").rearrange("p (a n) -> p a n", a=1)[:, :, bass.ds(r * P, DEC_T)]
                   .to_broadcast([P, DEC_B, DEC_T]), ALU.mult)\
                    .then_inc(rt_free[0], 1)
                b = group(3)
                dmat = const("dmat").rearrange("p (r n) -> p r n", n=P)[:, bass.ds(r, 1), :].to_broadcast([P, QBLK, P])
                tt(krt[:, :].rearrange("p (t n) -> p t n", n=P), b[:, :].rearrange("p (t n) -> p t n", n=P), dmat,
                   ALU.mult).then_inc(rt_free[1], 1)
                output_sum(0)
                decay = const("cdec")[:, bass.ds(r * 2, 1)]
                dve.wait_ge(states_out, r + 1)
                b = group(4)
                own.after(dve.tensor_copy(schain[:, 0, :], b[:, 0:RV]))
                dve.scalar_tensor_tensor(out=schain[:, 1, :], in0=schain[:, 0, :], scalar=decay, in1=b[:, RV:2 * RV],
                                         op0=ALU.mult, op1=ALU.add).then_inc(rt_free[0], 1)
                lows(1, 0, 0, 1)
                dve.wait_ge(rt_free[0], r * 9 + 4)
                b = group(5)
                own.after(dve.scalar_tensor_tensor(out=schain[:, 2, :], in0=schain[:, 1, :], scalar=decay,
                                                   in1=b[:, 0:RV], op0=ALU.mult, op1=ALU.add))
                dve.scalar_tensor_tensor(out=schain[:, 3, :], in0=schain[:, 2, :], scalar=decay,
                                         in1=b[:, RV:2 * RV], op0=ALU.mult, op1=ALU.add).then_inc(rt_free[1], 1)
                lows(1, 0, 1, 2)
                output(0)
                b = group(6)
                tt(atts[:, :], b[0:NS, 0:NS], const("dmats", NS)[:, bass.ds(r * NS, NS)], ALU.mult).then_inc(rt_free[0], 1)
                lows(1, 0, 2, TILES, [(7, lambda: queries_4_to_7(1))])
                rows(1)
                lows(1, 1, 0, 3)
                normalise_rows(1)
                prompt_statistics()
                b = group(9)
                dve.tensor_copy(qk[0:NS, QBLK, :], b[0:NS, 0:RV]).then_inc(rt_free[1], 1)
                sample_states(0)
                sample_states(1)
                sample_statistics()
                probs(1)
                sample_states(2)
                sample_states(3)
                lows(1, 1, 3, TILES)
                normalise()
                output_sum(1)
                for n in range(4):
                    b = group(14 + n)
                    e, lo, w = n % 2, (NS if n < 2 else 0), (SEQ if n < 2 else NS)
                    o = yb[:, bass.ds(r * (2 * NTOK) + (e * NTOK + lo), w)]
                    dve.scalar_tensor_tensor(out=o, in0=b[:, 0:w], scalar=gn[:, bass.ds(r * 2 + e, 1)], in1=o,
                                             op0=ALU.mult, op1=ALU.mult).then_inc(rt_free[n % 2], 1)
                output(1)

            with dve.Fori(0, RH) as r:
                own.enter(r, 15)
                retention_head(r)
            own.leave(RH)
            dve.wait_ge(co_read, 2 * RH + 1)
            dve.sem_inc(b_end, 1)
            dve.wait_ge(b_end, 4)

            dve.wait_ge(w_low, 2 * C0_C + 4)
            for n, (lo, src, hi) in enumerate(((oal, oa, oah), (ybl, yb, ybh))):
                dve.wait_ge(split_h, n + 1)
                tt(lo[:, :, :].rearrange("p k n -> p (k n)"), src[:, :],
                   hi[:, :, :].rearrange("p k n -> p (k n)").bitcast(F32), ALU.subtract).then_inc(split_l, 1)
            with dve.Fori(0, KT_N) as f:
                own.enter(f, 1)
                low(f * C_CH + (C0_C + 1), 1, 6 * P)
                dve.wait_ge(gt_free, f * 4 + 8)
                for u in range(4):
                    if u == 2:
                        low(f * C_CH + (C0_C + 2), 0)
                    dve.wait_ge(br_done, f * 4 + (u + 2))
                    s = slice((u % 2) * HALF, (u % 2 + 1) * HALF)
                    tt(uc[:, u // 2, s], bank[4 + u][:, 0:HALF], sgc[:, u // 2, s], ALU.mult).then_inc(br_free, 1)
                dve.wait_ge(br_free, f * 4 + 8)
                tt(uc[:, 0, :], uc[:, 0, :], uc[:, 1, :], ALU.add).then_inc(u_done, 1)
                dve.wait_ge(uh_done, f + 1)
                own.after(tt(ul[:, bass.ds(f, 1), :].rearrange("p k n -> p (k n)"), uc[:, 0, :],
                             uh[:, bass.ds(f, 1), :].rearrange("p k n -> p (k n)").bitcast(F32), ALU.subtract))
            own.leave(KT_N)
            dve.sem_inc(ul_done, KT_N)

            def normalise(t):
                m = P if t < QBLK else NS
                dve.wait_ge(zrstd_done, t + 1)
                own.after(dve.tensor_scalar(z[0:m, t, :], z[0:m, t, :], zmv[0:m, t, 0:1], zrs[0:m, t:t + 1],
                                            ALU.subtract, ALU.mult))
                own.after(tt(z[0:m, t, :], z[0:m, t, :], lng[0:m, :], ALU.mult))
                tt(z[0:m, t, :], z[0:m, t, :], lnb[0:m, :], ALU.add).then_inc(y_done, 1)

            dve.wait_ge(z_in, 32)
            dve.wait_ge(ln_in, 32)
            for n in range(4):
                if n < 3:
                    low(C0_O + n + 1, (n + 1) % 2)
                for t in range(TT):
                    v = n * TT + t
                    m = P if t < QBLK else NS
                    dve.wait_ge(ou_done, v + 1)
                    o = z[0:m, t, n * CW:(n + 1) * CW]
                    dve.scalar_tensor_tensor(out=o, in0=o, scalar=ALPHA, in1=bank[v % 8][0:m, 0:CW],
                                             op0=ALU.mult, op1=ALU.add).then_inc(ou_free, 1)
                    if n == 3:
                        dve.wait_ge(ou_free, v + 1)
                        for x in range(2):
                            i = dve.bn_stats(zst[0:m, t, 6 * x:6 * x + 6], z[0:m, t, 512 * x:512 * x + 512])
                        own.after(i)
                        dve.bn_aggr(zmv[0:m, t, :], zst[0:m, t, :]).then_inc(zvar_done, 1)
                        if t:
                            normalise(t - 1)
            normalise(TT - 1)


_INS = ["x_prompt", "x_sample", "cache_kv_w128", "cache_kv_w512", "cache_kv_w2048", "state_ret", "w_in", "w_pa",
        "w_pb", "w_o", "gn_g", "ln_g", "ln_b"]
_OUTS = ([(1, SEQ, D_MODEL), (DEC_B, DEC_T, D_MODEL)] + [(1, min(w, SEQ), 2, H, DH) for w, _ in GROUPS]
         + [(1, RH, RK, RV)] + [(DEC_B, w, 2, H, DH) for w, _ in GROUPS] + [(DEC_B, RH, RK, RV)])


def kernel(**inputs):
    import numpy as _np
    import concourse.bacc as _bacc
    from concourse import mybir as _mybir
    from concourse.bass_utils import run_bass_kernel_spmd as _run

    nc = _bacc.Bacc("TRN2", target_bir_lowering=False, num_devices=1)
    arrays = {name: _np.ascontiguousarray(inputs[name]) for name in _INS}
    arrays["gn_g"] = _np.ascontiguousarray(arrays["gn_g"].reshape(-1, P).T)
    arrays["consts"], arrays["dist_tab"] = shape_constants()
    arrays = {f"in_{name}_dram": a for name, a in arrays.items()}
    args = [nc.dram_tensor(name, a.shape, _mybir.dt.from_np(a.dtype), kind="ExternalInput").ap()
            for name, a in arrays.items()]
    for i, shape in enumerate(_OUTS):
        args.append(nc.dram_tensor(f"out_{i}_dram", shape, F32, kind="ExternalOutput").ap())
    bass_hybrid_step(nc, *args)
    r = _run(nc, [arrays], core_ids=[0])
    return tuple(r.results[0][f"out_{i}_dram"] for i in range(len(_OUTS)))
```
